# Optimizing a Trainium2 kernel written in Bass

```python
import jax, jax.numpy as jnp
from jax import lax
import numpy as np

D_MODEL = 2048
BATCH = 1
SEQ = 256
DEPTH = 2

CHUNK = 64
N_MIXERS = 2
N_GMLP_LAYERS = (DEPTH + N_MIXERS - 1) // N_MIXERS
N_SWA_LAYERS = DEPTH // N_MIXERS
GM_BLOCK = 128
GM_EXPAND = 6
GM_WIDTH = GM_EXPAND * D_MODEL // 2
GM_GROUPS = 8
GM_GROUP_DIM = GM_WIDTH // GM_GROUPS
HEAD_DIM = 64
N_Q_HEADS = D_MODEL // HEAD_DIM
N_KV_HEADS = N_Q_HEADS // 8
Q_PER_KV = N_Q_HEADS // N_KV_HEADS
ATT_WIDTH = N_Q_HEADS * HEAD_DIM
QKV_WIDTH = (N_Q_HEADS + 2 * N_KV_HEADS) * HEAD_DIM
WINDOW = 128
WINDOW_CHUNKS = WINDOW // CHUNK
ROPE_THETA = 10000.0
D_FF = ((8 * D_MODEL // 3 + 255) // 256) * 256
N_MOD = 6
RMS_EPS = 1e-6
LN_EPS = 1e-5

kernel_name = "hybrid_gmlp_swa_sink_adaln_trunk"

def rms_norm(x, g):
    xf = x.astype(jnp.float32)
    y = xf * lax.rsqrt(jnp.mean(xf * xf, axis=-1, keepdims=True) + RMS_EPS)
    return y.astype(x.dtype) * g

def layer_norm(x, g, b):
    xf = x.astype(jnp.float32)
    mu = jnp.mean(xf, axis=-1, keepdims=True)
    xc = xf - mu
    y = xc * lax.rsqrt(jnp.mean(xc * xc, axis=-1, keepdims=True) + LN_EPS)
    return y.astype(x.dtype) * g + b

def rope_tables(seq, dtype):
    inv_freq = 1.0 / (ROPE_THETA ** (jnp.arange(0, HEAD_DIM, 2, dtype=jnp.float32) / HEAD_DIM))
    pos = jnp.arange(seq, dtype=jnp.float32)
    ang = pos[:, None] * inv_freq[None, :]
    return jnp.cos(ang).astype(dtype), jnp.sin(ang).astype(dtype)

def apply_rope(x, cos, sin):
    x1, x2 = jnp.split(x, 2, axis=-1)
    c = cos[None, :, None, :]
    s = sin[None, :, None, :]
    return jnp.concatenate([x1 * c - x2 * s, x2 * c + x1 * s], axis=-1)

def gmlp_mixer(h, w_in, b_in, ln_g, ln_b, w_s, b_s, w_out):
    B, S, _ = h.shape
    z = jax.nn.gelu(h @ w_in + b_in, approximate=False)
    u, v = jnp.split(z, 2, axis=-1)
    v = layer_norm(v, ln_g, ln_b)
    nb = S // GM_BLOCK
    v = v.reshape(B, nb, GM_BLOCK, GM_GROUPS, GM_GROUP_DIM)
    cidx = jnp.arange(GM_BLOCK) // CHUNK
    causal = cidx[None, :] <= cidx[:, None]
    ws = jnp.where(causal[None], w_s, jnp.zeros_like(w_s))
    mixed = jnp.einsum('gij,bnjgc->bnigc', ws, v) + b_s.T[None, None, :, :, None]
    out = u * mixed.reshape(B, S, GM_WIDTH)
    return out @ w_out

def make_band(xc):
    nC = xc.shape[1]
    xp = jnp.pad(xc, ((0, 0), (WINDOW_CHUNKS - 1, 0), (0, 0), (0, 0), (0, 0)))
    return jnp.concatenate([xp[:, i:i + nC] for i in range(WINDOW_CHUNKS)], axis=2)

def swa_sink_attention(h, w_qkv, b_qkv, sinks, w_o, b_o, cos, sin):
    B, S, _ = h.shape
    nC = S // CHUNK
    qkv = h @ w_qkv + b_qkv
    q, k, v = jnp.split(qkv, [ATT_WIDTH, ATT_WIDTH + N_KV_HEADS * HEAD_DIM], axis=-1)
    q = apply_rope(q.reshape(B, S, N_Q_HEADS, HEAD_DIM), cos, sin)
    k = apply_rope(k.reshape(B, S, N_KV_HEADS, HEAD_DIM), cos, sin)
    v = v.reshape(B, S, N_KV_HEADS, HEAD_DIM)
    q = q.reshape(B, nC, CHUNK, N_KV_HEADS, Q_PER_KV, HEAD_DIM)
    k_band = make_band(k.reshape(B, nC, CHUNK, N_KV_HEADS, HEAD_DIM))
    v_band = make_band(v.reshape(B, nC, CHUNK, N_KV_HEADS, HEAD_DIM))
    s = jnp.einsum('bcqgrd,bckgd->bcgrqk', q, k_band).astype(jnp.float32) * (HEAD_DIM ** -0.5)
    key_chunk = jnp.arange(nC)[:, None] - (WINDOW_CHUNKS - 1) + jnp.arange(WINDOW_CHUNKS * CHUNK)[None, :] // CHUNK
    valid = key_chunk >= 0
    s = jnp.where(valid[None, :, None, None, None, :], s, -jnp.inf)
    sink = jnp.broadcast_to(
        sinks.astype(jnp.float32).reshape(N_KV_HEADS, Q_PER_KV)[None, None, :, :, None, None],
        s.shape[:-1] + (1,))
    p = jax.nn.softmax(jnp.concatenate([s, sink], axis=-1), axis=-1)[..., :-1]
    o = jnp.einsum('bcgrqk,bckgd->bcqgrd', p.astype(v.dtype), v_band)
    return o.reshape(B, S, ATT_WIDTH) @ w_o + b_o

def swiglu(h, w_gu, w_down):
    g, u = jnp.split(h @ w_gu, 2, axis=-1)
    return (jax.nn.silu(g) * u) @ w_down

def setup_inputs(seed: int = 0) -> dict:
    key = jax.random.key(seed)
    ks = jax.random.split(key, 24)
    f32 = jnp.float32
    L, NA, NB, D, E = DEPTH, N_GMLP_LAYERS, N_SWA_LAYERS, D_MODEL, GM_WIDTH
    n = lambda k, shape, s: jax.random.normal(k, shape, f32) * s
    return {
        "x": n(ks[0], (BATCH, SEQ, D), 1.0),
        "c": n(ks[1], (BATCH, D), 1.0),
        "ada_w": n(ks[2], (L, D, N_MOD * D), 0.5 * D ** -0.5),
        "ada_b": n(ks[3], (L, N_MOD * D), 0.02),
        "mix_norm_g": 1.0 + n(ks[4], (L, D), 0.05),
        "ffn_norm_g": 1.0 + n(ks[5], (L, D), 0.05),
        "gm_w_in": n(ks[6], (NA, D, 2 * E), D ** -0.5),
        "gm_b_in": n(ks[7], (NA, 2 * E), 0.02),
        "gm_ln_g": 1.0 + n(ks[8], (NA, E), 0.05),
        "gm_ln_b": n(ks[9], (NA, E), 0.02),
        "gm_w_s": n(ks[10], (NA, GM_GROUPS, GM_BLOCK, GM_BLOCK), GM_BLOCK ** -0.5),
        "gm_b_s": 1.0 + n(ks[11], (NA, GM_GROUPS, GM_BLOCK), 0.1),
        "gm_w_out": n(ks[12], (NA, E, D), E ** -0.5),
        "sw_w_qkv": n(ks[13], (NB, D, QKV_WIDTH), D ** -0.5),
        "sw_b_qkv": n(ks[14], (NB, QKV_WIDTH), 0.02),
        "sw_sinks": n(ks[15], (NB, N_Q_HEADS), 0.5),
        "sw_w_o": n(ks[16], (NB, ATT_WIDTH, D), ATT_WIDTH ** -0.5),
        "sw_b_o": n(ks[17], (NB, D), 0.02),
        "ffn_w_gu": n(ks[18], (L, D, 2 * D_FF), D ** -0.5),
        "ffn_w_down": n(ks[19], (L, D_FF, D), D_FF ** -0.5),
        "final_g": 1.0 + n(ks[20], (D,), 0.05),
    }

def reference(x, c, ada_w, ada_b, mix_norm_g, ffn_norm_g, gm_w_in, gm_b_in, gm_ln_g, gm_ln_b,
              gm_w_s, gm_b_s, gm_w_out, sw_w_qkv, sw_b_qkv, sw_sinks, sw_w_o, sw_b_o,
              ffn_w_gu, ffn_w_down, final_g):
    S = x.shape[1]
    cos, sin = rope_tables(S, x.dtype)
    cond = jax.nn.silu(c)
    for layer in range(DEPTH):
        mod = (cond @ ada_w[layer] + ada_b[layer])[:, None, :]
        sh1, sc1, g1, sh2, sc2, g2 = jnp.split(mod, N_MOD, axis=-1)
        h = rms_norm(x, mix_norm_g[layer]) * (1.0 + sc1) + sh1
        j = layer // N_MIXERS
        if layer % N_MIXERS == 0:
            y = gmlp_mixer(h, gm_w_in[j], gm_b_in[j], gm_ln_g[j], gm_ln_b[j],
                           gm_w_s[j], gm_b_s[j], gm_w_out[j])
        else:
            y = swa_sink_attention(h, sw_w_qkv[j], sw_b_qkv[j], sw_sinks[j],
                                   sw_w_o[j], sw_b_o[j], cos, sin)
        x = x + g1 * y
        h = rms_norm(x, ffn_norm_g[layer]) * (1.0 + sc2) + sh2
        x = x + g2 * swiglu(h, ffn_w_gu[layer], ffn_w_down[layer])
    return rms_norm(x, final_g)


_drawn_inputs = setup_inputs


def setup_inputs(seed=0):
    import zlib

    import numpy as np

    out = dict(_drawn_inputs(seed))
    spreads = {}
    factors = {'mix_norm_g': 3.094,
     'ffn_norm_g': 2.7,
     'gm_b_in': 8.0,
     'gm_ln_g': 5.94,
     'gm_ln_b': 8.0,
     'sw_b_qkv': 8.0,
     'sw_sinks': 64.0,
     'sw_b_o': 34.524}
    for name, (base, spread) in spreads.items():
        noise = np.random.default_rng([zlib.crc32(name.encode()), seed]).standard_normal(out[name].shape)
        drawn = base * np.exp(spread * noise) if base else spread * noise
        out[name] = __import__('jax').numpy.asarray(drawn.astype(out[name].dtype))
    for name, factor in factors.items():
        out[name] = (out[name] * factor).astype(out[name].dtype)
    return out
```

```python
from contextlib import ExitStack

import concourse.bass as bass
from concourse import mybir

F32 = mybir.dt.float32
F32R = mybir.dt.float32r
BF16 = mybir.dt.bfloat16
ALU = mybir.AluOpType
ACT = mybir.ActivationFunctionType
AX = mybir.AxisListType

P = 128
WG, WU, WD = 0, 2, 4
ADA_BANK = {"start": 7, "v": 7, "u": 0, "ffn": 2}
EPS_RMS, EPS_LN = 1e-6, 1e-5


def w_order(n_w, n_ada):
    order = []
    for q in range(n_w):
        order.append(("W", q))
        if q < n_ada:
            order.append(("A", q))
    return order + [("A", q) for q in range(n_w, n_ada)]


class Piece:

    def __init__(self, n_w, n_ada, turn, unit, ada, reps=1):
        self.order = w_order(n_w, n_ada)
        self.n_w, self.n_ada, self.reps = n_w, n_ada, reps
        self.turn0, self.unit0, self.ada0 = turn, unit, ada
        self.pos = {k: e for e, k in enumerate(self.order)}

    def turn(self, i=0):
        return self.turn0 + i * (len(self.order) // 4)

    def unit(self, i=0):
        return self.unit0 + i * (2 * self.n_w)

    def ada(self, i=0):
        return self.ada0 + i * (self.n_ada // 4)

    def after(self):
        return self.turn(self.reps), self.unit(self.reps), self.ada(self.reps)


def trunk(nc, x, c, ada_w, ada_b, mix_norm_g, ffn_norm_g, gm_w_in, gm_b_in, gm_ln_g, gm_ln_b, gm_w_s,
          gm_b_s, gm_w_out, sw_w_qkv, sw_b_qkv, sw_sinks, sw_w_o, sw_b_o, ffn_w_gu, ffn_w_down, final_g,
          consts, mask_consts, out):
    D = x.shape[2]
    KD = D // P
    E = gm_w_out.shape[1]
    FF = ffn_w_down.shape[1]
    GM_STEPS, FF_STEPS = E // 512, FF // 512
    ET = E // P
    GROUPS = gm_w_s.shape[1]
    TPG = ET // GROUPS
    NQ = sw_sinks.shape[1]
    ATT = NQ * 64
    KV = (sw_w_qkv.shape[2] - ATT) // 2
    assert D == 2048 and x.shape[1] == 256 and KV == 256 and ATT == 2048 and GM_STEPS == 12 and FF_STEPS == 11

    at = (0, 0, 0)
    pieces = {}
    for name, n_w, n_ada, reps in (
            ("start", 0, 8, 4), ("v0", 8, 4, 1), ("v", 8, 4, 5), ("u_pro", 8, 0, 1), ("u_first", 8, 4, 1),
            ("u", 8, 4, 9), ("u_epi", 8, 0, 1),
            ("f0_pro", 12, 8, 1), ("f0", 12, 8, 9), ("f0_epi", 12, 8, 1),
            ("qkv", 20, 0, 1), ("wo", 16, 0, 1),
            ("f1_pro", 12, 8, 1), ("f1", 12, 0, 9), ("f1_epi", 12, 0, 1)):
        pieces[name] = Piece(n_w, n_ada, *at, reps=reps)
        at = pieces[name].after()
    S = pieces
    STEP_F = (GM_STEPS, GM_STEPS + FF_STEPS)
    EV_F = (8 * GM_STEPS, 8 * (GM_STEPS + FF_STEPS) + 8)
    EV_WO = 8 * (GM_STEPS + FF_STEPS)
    EV_END = EV_F[1] + 8 * FF_STEPS

    ROOT, ROOT_LN = (1, 3, 4, 5, 6), 2

    with ExitStack() as ctx:
        def sb(name, shape, dt):
            return ctx.enter_context(nc.sbuf_tensor(name, shape, dt))

        def sem(name):
            return ctx.enter_context(nc.semaphore(name))

        xs = sb("xs", [P, 2, D], F32)
        hTh = sb("hTh", [P, KD, 256], F32R)
        hTl = sb("hTl", [P, KD, 256], F32R)
        big = sb("big", [P, ET * 256], F32)
        hidh = sb("hidh", [P, 4, 256], F32R)
        hidl = sb("hidl", [P, 4, 256], F32R)
        hid = sb("hid", [P, 4, 256], F32)
        raw = sb("raw", [P, 4, 4, 512], F32)
        whi = sb("whi", [P, 4, 2, 512], F32R)
        wlo = sb("wlo", [P, 4, 2, 512], F32R)
        gate = sb("gate", [P, D], F32)
        acc = sb("acc", [P, 2, 512], F32)
        tmp = sb("tmp", [P, 2, 512], F32)
        ident = sb("ident", [P, P], F32)
        ones = sb("ones", [P, P], F32)
        wsT = sb("wsT", [P, GROUPS, P], F32)
        rs_bc = sb("rs_bc", [P, GROUPS, P], F32)
        bs_bc = sb("bs_bc", [P, GROUPS, P], F32)
        cols = sb("cols", [P, 5, P], F32)
        mod = sb("mod", [P, 2 * 96], F32)
        ccol = sb("ccol", [P, KD], F32)
        amul = sb("amul", [P, KD], F32)
        small = sb("small", [P, 64], F32)
        vst = sb("vst", [P, 2, GM_STEPS, 6], F32)
        negsink = sb("negsink", [P, NQ], F32)
        stat = sb("stat", [P, 7, 2, 8], F32)
        maskc = sb("maskc", [2, 512], BF16)
        ps = ctx.enter_context(nc.psum_tensor("ps", [P, 8, 512], F32))

        vT = big[:, :].rearrange("p (c b i) -> p c b i", b=2, i=P)
        nrm = big[:, 0:2 * D].rearrange("p (b d) -> p b d", b=2)
        nat = big[:, 4096:4736].rearrange("p (t i) -> p t i", t=5)
        wsn = big[:, 5120:6144].rearrange("p (g j) -> p g j", g=GROUPS)
        qT = big[:, 0:4096].rearrange("p (t q) -> p t q", t=16)
        kT = big[:, 4096:4608].rearrange("p (t q) -> p t q", t=2)
        kdup = big[:, 4608:5632].rearrange("p (g q) -> p g q", g=4)
        vtok = big[:, 5632:6144].rearrange("p (b d) -> p b d", b=2)
        prob = big[:, 6144:9216].rearrange("p (s n) -> p s n", s=2)
        probT = big[:, 9216:10752].rearrange("p (r h q) -> p r h q", r=3, h=4)
        trig = big[:, 10752:11264].rearrange("p (t q) -> p t q", t=2)
        rot = big[:, 11264:11392]
        vb_bc = big[:, 11392:11648]
        rtmp = big[:, 11648:12160].rearrange("p (t q) -> p t q", t=2)
        outs = big[:, 4096:8192].rearrange("p (b d) -> p b d", b=2)
        fg_bc = big[:, 8192:8192 + D]

        mask32 = big[0:2, 6144:6656]

        C0, MIXG, FFNG, BQKV, BO = 0, 16, 48, 80, 100
        adab = cols[:, 1:3, 0:96]
        bu, lng, lnb = cols[:, 3, 0:48], cols[:, 3, 48:96], cols[:, 4, 0:48]

        raw_landed = [sem(f"raw_landed{i}") for i in range(4)]
        raw_used = sem("raw_used")
        hi_ready = sem("hi_ready")
        unit_done = sem("unit_done")
        ada_reduced = sem("ada_reduced")
        mod_ready = sem("mod_ready")
        vec_landed = sem("vec_landed")
        x_landed = sem("x_landed")
        bs_landed = sem("bs_landed")
        nat_zero = sem("nat_zero")
        ones_ready = sem("ones_ready")
        turned = sem("turned")
        table = sem("table")
        cond_ready = sem("cond_ready")
        ws_ready = sem("ws_ready")
        sq_ready = sem("sq_ready")
        sq_step = sem("sq_step")
        ms_ready = sem("ms_ready")
        root_ready = sem("root_ready")
        n_ready = sem("n_ready")
        nT_ready = sem("nT_ready")
        h_ready = sem("h_ready")
        hT_hi = sem("hT_hi")
        hT_ready = sem("hT_ready")
        vb_landed = [sem(f"vb_landed{i}") for i in range(2)]
        v_biased = sem("v_biased")
        v_gelu = sem("v_gelu")
        v_stats = sem("v_stats")
        v_normed = sem("v_normed")
        mix_done = sem("mix_done")
        mix_t = sem("mix_t")
        mixed = sem("mixed")
        gelu_u = sem("gelu_u")
        silu_g = sem("silu_g")
        hid_ready = sem("hid_ready")
        hid_hi = sem("hid_hi")
        hid_lo = sem("hid_lo")
        out_evac = sem("out_evac")
        x_added = sem("x_added")
        diag_ready = sem("diag_ready")
        bc_done = sem("bc_done")
        gate_evac = sem("gate_evac")
        bo_added = sem("bo_added")
        dve_step = sem("dve_step")
        att_landed = sem("att_landed")
        q_bias = sem("q_bias")
        rot_done = sem("rot_done")
        roped = sem("roped")
        dup_done = sem("dup_done")
        dup_ready = sem("dup_ready")
        vtok_ready = sem("vtok_ready")
        s_done = sem("s_done")
        s_even = sem("s_even")
        s_max = sem("s_max")
        p_exp = sem("p_exp")
        p_norm = sem("p_norm")
        pt_done = sem("pt_done")
        pt_a = sem("pt_a")
        pt_v = sem("pt_v")
        o_done = sem("o_done")
        o_hi = sem("o_hi")
        o_lo = sem("o_lo")
        fg_landed = sem("fg_landed")
        out_ready = sem("out_ready")
        stored = sem("stored")

        block = ctx.enter_context(nc.Block())

        w_in, w_out = gm_w_in[0], gm_w_out[0]
        w_qkv, w_o = sw_w_qkv[0], sw_w_o[0]

        def tile_of(w, rows, col):
            return w[bass.ds(rows, 512), bass.ds(col, 512)].rearrange("(k p) n -> p k n", p=P)

        @block.sync
        def _(sp):
            def load(piece, i, q_src, ada_src):
                for e, (kind, q) in enumerate(piece.order):
                    turn = piece.turn(i)
                    if not (isinstance(turn, int) and 4 * turn + e < 4):
                        sp.wait_ge(raw_used, 16 * turn + 4 * e - 12)
                    src = q_src(q) if kind == "W" else ada_src(q)
                    sp.dma_start(raw[:, e % 4], src).then_inc(raw_landed[e % 4], 16)

            def ada_at(layer, unit):
                return lambda q: tile_of(ada_w[layer], 512 * (q % 4), (unit + q // 4) * 512)

            def v_src(i):
                return lambda q: tile_of(w_in, 512 * (q % 4), E + (2 * i + q // 4) * 512)

            def u_grp(j, q):
                return tile_of(w_in, 512 * q, j * 512)

            def out_grp(w, j, q):
                return tile_of(w, j * 512, 512 * q)

            def gate_grp(l, j, q):
                return tile_of(ffn_w_gu[l], 512 * q, j * 512)

            def up_grp(l, j, q):
                return tile_of(ffn_w_gu[l], 512 * q, FF + j * 512)

            load(S["start"], 0, None, ada_at(0, 0))
            with sp.Fori(1, 4) as i:
                load(S["start"], i, None, ada_at(0, 2 * i))
            load(S["v0"], 0, v_src(0), ada_at(0, 8))
            with sp.Fori(0, 5) as i:
                load(S["v"], i, v_src(i + 1), ada_at(0, i + 9))
            load(S["u_pro"], 0, lambda q: u_grp(q // 4, q % 4), None)

            def u_body(piece, i, j):
                load(piece, i, lambda q: out_grp(w_out, j - 1, q) if q < 4 else u_grp(j + 1, q - 4),
                     ada_at(0, j + 13))
            u_body(S["u_first"], 0, 1)
            with sp.Fori(0, 9) as i:
                u_body(S["u"], i, i + 2)
            load(S["u_epi"], 0, lambda q: out_grp(w_out, GM_STEPS - 2 + q // 4, q % 4), None)

            def ffn(l, tag, a_pro, a_loop, a_epi):
                def body(j):
                    def src(q):
                        if q < 4:
                            return up_grp(l, j, q)
                        if q < 8:
                            return out_grp(ffn_w_down[l], j - 1, q - 4)
                        return gate_grp(l, j + 1, q - 8)
                    return src

                def epi(q):
                    if q < 4:
                        return up_grp(l, FF_STEPS - 1, q)
                    return out_grp(ffn_w_down[l], FF_STEPS - 3 + q // 4, q % 4)
                load(S[tag + "_pro"], 0, lambda q: gate_grp(l, 0, q) if q < 4 else
                     up_grp(l, 0, q - 4) if q < 8 else gate_grp(l, 1, q - 8), ada_at(1, a_pro))
                with sp.Fori(0, 9) as i:
                    load(S[tag], i, body(i + 1), ada_at(1, a_loop(i)))
                load(S[tag + "_epi"], 0, epi, ada_at(1, a_epi))

            ffn(0, "f0", 0, lambda i: 2 * i + 2, 20)
            load(S["qkv"], 0, lambda q: tile_of(w_qkv, 512 * (q % 4), 512 * (q // 4)), None)
            load(S["wo"], 0, lambda q: tile_of(w_o, 512 * (q % 4), 512 * (q // 4)), None)
            ffn(1, "f1", 22, lambda i: 0, 0)
            for b in range(2):
                sp.wait_ge(out_ready, b + 1)
                sp.dma_start(out[0, b * P:(b + 1) * P, :], outs[:, b, :]).then_inc(stored, 16)
            sp.wait_ge(stored, 32)

        @block.gpsimd
        def _(pool):
            def bias_rows(t):
                for slot in range(2):
                    if not (isinstance(t, int) and t == 0):
                        pool.wait_ge(v_biased, 4 * t + 2 * slot - 2)
                    pool.dma_start(tmp[:, slot, :], gm_b_in[0, bass.ds(E + (2 * t + slot) * 512, 512)]
                                   .partition_broadcast(P)).then_inc(vb_landed[slot], 16)
            bias_rows(0)
            with pool.Fori(1, GM_STEPS // 2) as i:
                bias_rows(i)

            def add_outputs(n0):
                for k in range(8):
                    pool.wait_ge(out_evac, n0 + k + 1)
                    nc.gpsimd.tensor_tensor(xs[:, k % 2, (k // 2) * 512:(k // 2 + 1) * 512],
                                            xs[:, k % 2, (k // 2) * 512:(k // 2 + 1) * 512],
                                            tmp[:, k % 2, :], ALU.add).then_inc(x_added, 1)
            with pool.Fori(0, EV_END // 8) as i:
                add_outputs(8 * i)

        @block.scalar
        def _(act):
            act.dma_start(ident[:], consts[:, 0:128]).then_inc(vec_landed, 16)
            act.wait_ge(nat_zero, 1)
            small_loads = [
                (nat[0:16, 0, :], c[0].rearrange("(r i) -> r i", i=P)),
                (nat[16:48, 0, :], mix_norm_g.rearrange("l (r i) -> (l r) i", i=P)),
                (nat[48:80, 0, :], ffn_norm_g.rearrange("l (r i) -> (l r) i", i=P)),
                (nat[80:100, 0, :], sw_b_qkv[0].rearrange("(r i) -> r i", i=P)),
                (nat[100:116, 0, :], sw_b_o[0].rearrange("(r i) -> r i", i=P)),
                (nat[0:96, 1, :], ada_b[0].rearrange("(r i) -> r i", i=P)),
                (nat[0:96, 2, :], ada_b[1].rearrange("(r i) -> r i", i=P)),
                (nat[0:48, 3, :], gm_b_in[0, 0:E].rearrange("(r i) -> r i", i=P)),
                (nat[48:96, 3, :], gm_ln_g[0].rearrange("(r i) -> r i", i=P)),
                (nat[0:48, 4, :], gm_ln_b[0].rearrange("(r i) -> r i", i=P)),
                (wsn, gm_w_s[0].rearrange("g i j -> i g j")),
                (negsink[:, :], sw_sinks[0].partition_broadcast(P)),
                (mask32, mask_consts),
            ]
            for dst, src in small_loads:
                act.dma_start(dst, src).then_inc(vec_landed, 16)
            act.dma_start(xs[:, :, :], x[0].rearrange("(b p) d -> p b d", p=P)).then_inc(x_landed, 16)
            act.dma_start(bs_bc[:, :, :].rearrange("p g i -> p (g i)"),
                          gm_b_s[0].rearrange("g i -> (g i)").partition_broadcast(P)).then_inc(bs_landed, 16)
            act.wait_ge(turned, 1)
            nc.scalar.copy(cols[:, 0, :], ps[:, 6, 0:128]).then_inc(table, 1)
            act.wait_ge(table, 1)
            nc.scalar.activation(ccol[:, :], cols[:, 0, C0:C0 + KD], ACT.Silu).then_inc(cond_ready, 1)
            act.wait_ge(turned, 2)
            nc.scalar.copy(cols[:, 1:5, :], ps[:, 5, :].rearrange("p (t i) -> p t i", t=4)).then_inc(table, 1)

            def stage_hi(piece, i, e, q):
                act.wait_ge(raw_landed[e % 4], 16 * (piece.turn(i) + e // 4 + 1))
                for h in range(2):
                    u = piece.unit(i) + 2 * q + h
                    if not (isinstance(u, int) and u < 4):
                        act.wait_ge(unit_done, u - 3)
                    nc.scalar.copy(whi[:, (2 * q + h) % 4], raw[:, e % 4, 2 * h:2 * h + 2, :]).then_inc(hi_ready, 1)

            def stage(piece, i, q):
                stage_hi(piece, i, piece.pos[("W", q)], q)

            def root(n):
                act.wait_ge(ms_ready, n)
                nc.scalar.activation(small[:, 12:14], small[:, 10:12], ACT.Sqrt).then_inc(root_ready, 1)

            def norm_stats(k, n_last):
                for m in range(8):
                    ch, b = m // 2, m % 2
                    if n_last is not None:
                        act.wait_ge(x_added, n_last + m + 1)
                    elif m == 0:
                        act.wait_ge(x_landed, 16)
                    nc.scalar.activation(hid[:, 0:2, :], xs[:, b, ch * 512:(ch + 1) * 512].rearrange(
                        "p (a c) -> p a c", a=2), ACT.Square, accum_out=small[:, b * 4 + ch:b * 4 + ch + 1]
                    ).then_inc(sq_ready, 1)
                    act.wait_ge(sq_ready, 8 * k + m + 1)
                root(ROOT[k])

            def norm_hi(k, q):
                for kt in range(4 * q, 4 * q + 4):
                    act.wait_ge(h_ready, 16 * k + kt + 1)
                    nc.scalar.copy(hTh[:, kt, :], hid[:, kt % 4, :]).then_inc(hT_hi, 1)

            def split_hi(step, units):
                if units is not None:
                    act.wait_ge(unit_done, units)
                for m in range(2):
                    act.wait_ge(hid_ready, 2 * step + m + 1)
                    nc.scalar.copy(hidh[:, 2 * m:2 * m + 2, :], hid[:, 2 * m:2 * m + 2, :]).then_inc(hid_hi, 1)

            def gate_rows(b, events):
                if events:
                    act.wait_ge(out_evac, events)
                for ch in range(4):
                    act.wait_ge(bc_done, 4 * b + ch + 1)
                    nc.scalar.copy(gate[:, ch * 512:(ch + 1) * 512], ps[:, WD + ch, :]).then_inc(gate_evac, 1)

            act.wait_ge(turned, 3)
            nc.scalar.copy(wsT[:, :, :], ps[:, 3:5, :].rearrange("p k (g i) -> p (k g) i", i=P)).then_inc(table, 1)
            act.wait_ge(turned, 4)
            nc.scalar.copy(rs_bc[:, :, :], ps[:, 1:3, :].rearrange("p k (g i) -> p (k g) i", i=P)).then_inc(table, 1)

            norm_stats(0, None)

            def v_gelu_chunk(ch):
                for b in range(2):
                    act.wait_ge(v_biased, 2 * ch + b + 1)
                    vc = vT[:, bass.ds(4 * ch, 4), b, :]
                    nc.scalar.activation(vc, vc, ACT.Gelu).then_inc(v_gelu, 1)

            def v_body(piece, i, t, first):
                for q in range(8):
                    stage(piece, i, q)
                    if first and q < 4:
                        norm_hi(0, q)
                    if q == 0 and not first:
                        v_gelu_chunk(2 * t - 1)
                    if q == 4:
                        v_gelu_chunk(2 * t)
            v_body(S["v0"], 0, 0, True)
            with act.Fori(0, 5) as i:
                v_body(S["v"], i, i + 1, False)

            def u_gelu(j, units, split_before):
                act.wait_ge(unit_done, units)
                if split_before:
                    act.wait_ge(hid_lo, 2 * j)
                for m in range(4):
                    ins = nc.scalar.activation(hid[:, m, :], ps[:, WU + m // 2, (m % 2) * 256:(m % 2 + 1) * 256],
                                               ACT.Gelu, bias=bu[:, bass.ds(4 * j + m, 1)])
                    if m % 2:
                        ins.then_inc(gelu_u, 1)
            for q in range(8):
                stage(S["u_pro"], 0, q)
                if q == 0:
                    v_gelu_chunk(GM_STEPS - 1)
                if q == 1:
                    root(ROOT_LN)
                if q == 4:
                    u_gelu(0, S["u_pro"].unit() + 8, False)
                if q == 5:
                    split_hi(0, None)
            gate_rows(0, 0)

            def u_body(piece, i, j):
                for q in range(8):
                    stage(piece, i, q)
                    if q == 0:
                        u_gelu(j, piece.unit(i), True)
                    if q == 4:
                        split_hi(j, piece.unit(i) + 8)
            u_body(S["u_first"], 0, 1)
            with act.Fori(0, 9) as i:
                u_body(S["u"], i, i + 2)
            L = GM_STEPS - 1
            for q in range(8):
                stage(S["u_epi"], 0, q)
                if q == 0:
                    u_gelu(L, S["u_epi"].unit(), True)
                if q == 4:
                    split_hi(L, S["u_epi"].unit() + 8)

            def ffn(l, tag, k_norm):
                s0, n0 = STEP_F[l], EV_F[l]

                def silu(j, units, split_before):
                    act.wait_ge(unit_done, units)
                    if split_before:
                        act.wait_ge(hid_lo, 2 * (s0 + j))
                    for m in range(2):
                        nc.scalar.activation(hid[:, 2 * m:2 * m + 2, :].rearrange("p a c -> p (a c)"),
                                             ps[:, WG + m, :], ACT.Silu).then_inc(silu_g, 1)
                pro = S[tag + "_pro"]
                stage(pro, 0, 0)
                norm_stats(k_norm, n0 - 8)
                for q in range(12):
                    if q:
                        stage(pro, 0, q)
                    if q < 4:
                        norm_hi(k_norm, q)
                    if q == 4:
                        silu(0, pro.unit() + 8, False)
                    if q == 9:
                        split_hi(s0, None)
                gate_rows((1, 4)[l], n0)

                def body(i, j):
                    for q in range(12):
                        stage(S[tag], i, q)
                        if q == 0:
                            silu(j, S[tag].unit(i), True)
                        if q == 8:
                            split_hi(s0 + j, S[tag].unit(i) + 16)
                with act.Fori(0, 9) as i:
                    body(i, i + 1)
                for q in range(12):
                    stage(S[tag + "_epi"], 0, q)
                    if q == 0:
                        silu(FF_STEPS - 1, S[tag + "_epi"].unit(), True)
                    if q == 8:
                        split_hi(s0 + FF_STEPS - 1, S[tag + "_epi"].unit() + 16)

            ffn(0, "f0", 1)

            att_loads = [(trig, consts[:, 256:768].rearrange("p (t q) -> p t q", t=2)), (rot, consts[:, 128:256]),
                         (vb_bc, sw_b_qkv[0, ATT + KV:ATT + 2 * KV].partition_broadcast(P))]
            for dst, src in att_loads:
                act.dma_start(dst, src).then_inc(att_landed, 16)
            stage(S["qkv"], 0, 0)
            norm_stats(2, EV_WO - 8)

            def qk_bias(pair, bank):
                dst = qT if pair < 8 else kT
                for m in range(2):
                    ins = nc.scalar.activation(dst[:, (2 * pair) % 16 + m, :], ps[:, bank, m * 256:(m + 1) * 256],
                                               ACT.Identity, bias=cols[:, 0, BQKV + 2 * pair + m:BQKV + 2 * pair + m + 1])
                ins.then_inc(q_bias, 1)
            for q in range(20):
                if q:
                    stage(S["qkv"], 0, q)
                if q < 4:
                    norm_hi(2, q)
                if q >= 4 and q % 4 == 0:
                    for m in range(2):
                        pair = 2 * (q // 4 - 1) + m
                        act.wait_ge(unit_done, S["qkv"].unit() + 2 * q)
                        qk_bias(pair, 2 * ((q // 4 - 1) % 2) + m)
            act.wait_ge(unit_done, S["qkv"].unit() + 40)
            qk_bias(8, 0)
            for m in range(2):
                act.wait_ge(dup_done, m + 1)
                nc.scalar.copy(kdup[:, 2 * m:2 * m + 2, :], ps[:, 6 + m, :].rearrange("p (a q) -> p a q", a=2)
                               ).then_inc(dup_ready, 1)

            def exps(Q):
                s, bk = Q % 2, 3 * (Q % 2)
                if Q >= 2:
                    act.wait_ge(pt_done, 3 * (Q - 1))
                act.wait_ge(s_max, 2 * (Q + 1))
                for i in range(8):
                    mb, r = i // 4, i % 4
                    src = ps[:, bk, r * 128:(r + 1) * 128] if mb == 0 else \
                        ps[:, bk + 1 + r % 2, (r // 2) * 256:(r // 2 + 1) * 256]
                    dst = prob[:, s, r * 128:(r + 1) * 128] if mb == 0 else \
                        prob[:, s, 512 + r * 256:512 + (r + 1) * 256]
                    nc.scalar.activation(dst, src, ACT.Exp, bias=stat[:, 1, s, i:i + 1], scale=0.125,
                                         accum_out=stat[:, 3, s, i:i + 1]).then_inc(p_exp, 1)
                nc.scalar.activation(stat[:, 4, s, :], stat[:, 2, s, :], ACT.Exp).then_inc(p_exp, 1)

            def att_out(Q):
                bk = 3 * (Q % 2)
                if Q >= 1:
                    act.wait_ge(o_done, Q)
                for r in (1, 2):
                    act.wait_ge(pt_done, 3 * Q + r + 1)
                    nc.scalar.copy(probT[:, r], ps[:, bk + r, :].rearrange("p (h q) -> p h q", h=4)).then_inc(pt_a, 1)
                act.wait_ge(o_done, Q + 1)
                nc.scalar.copy(hTh[:, 2 * Q:2 * Q + 2, :], ps[:, 6 + Q % 2, :].rearrange("p (t q) -> p t q", t=2)
                               ).then_inc(o_hi, 1)
            NQD = NQ // 4
            exps(0)
            for Q in range(NQD):
                if Q + 1 < NQD:
                    exps(Q + 1)
                att_out(Q)
            gate_rows(2, EV_WO)
            for q in range(16):
                stage(S["wo"], 0, q)
            act.dma_start(fg_bc, final_g.partition_broadcast(P)).then_inc(fg_landed, 16)
            ffn(1, "f1", 3)
            norm_stats(4, EV_END - 8)

        @block.vector
        def _(dve):
            chain = [0]

            def link(ins):
                chain[0] += 1
                ins.then_inc(dve_step, 1)
                dve.wait_ge(dve_step, chain[0])

            nc.vector.memset(big[:, 4096:6144], 0.0).then_inc(nat_zero, 1)
            nc.vector.memset(ones[:], 1.0).then_inc(ones_ready, 1)

            def quarter(piece, i, e):
                return 16 * piece.turn(i) + 4 * e

            def stage_lo(piece, i, e, q):
                for h in range(2):
                    dve.wait_ge(hi_ready, piece.unit(i) + 2 * q + h + 1)
                    s = (2 * q + h) % 4
                    nc.vector.tensor_tensor(wlo[:, s], raw[:, e % 4, 2 * h:2 * h + 2, :], whi[:, s].bitcast(F32),
                                            ALU.subtract).then_inc(raw_used, 2)

            def ada_group(piece, i, e, q, two):
                dve.wait_ge(raw_landed[e % 4], 16 * (piece.turn(i) + e // 4 + 1))
                unit, slot = piece.ada(i) + q // 4, (q // 4) if two else 0
                if q % 4 == 0:
                    if not (isinstance(unit, int) and unit < 2):
                        dve.wait_ge(ada_reduced, unit - 1 if two else unit)
                for kk in range(4):
                    kt = 4 * (q % 4) + kk
                    if not (isinstance(unit, int) and unit == 0 and kt == 0):
                        dve.wait_ge(raw_used, quarter(piece, i, e) + kk)
                    if kt == 0:
                        ins = nc.vector.tensor_scalar(acc[:, slot, :], raw[:, e % 4, kk, :], ccol[:, 0:1], None, ALU.mult)
                    else:
                        ins = nc.vector.scalar_tensor_tensor(out=acc[:, slot, :], in0=raw[:, e % 4, kk, :],
                                                             scalar=ccol[:, kt:kt + 1], in1=acc[:, slot, :],
                                                             op0=ALU.mult, op1=ALU.add)
                    ins.then_inc(raw_used, 1)

            def mod_add(unit, layer, blk, n, bank):
                dve.wait_ge(ada_reduced, unit + n)
                dst = mod[:, bass.ds(96 * layer + 4 * blk, 4 * n)]
                nc.vector.tensor_tensor(dst, ps[:, bank, 0:4 * n],
                                        cols[:, 1 + layer, bass.ds(4 * blk, 4 * n)], ALU.add).then_inc(mod_ready, n)

            def run(piece, i, hooks, two):
                for e, (kind, q) in enumerate(piece.order):
                    if kind == "A":
                        ada_group(piece, i, e, q, two)
                    else:
                        stage_lo(piece, i, e, q)
                        hooks(q)

            def inverse_root(n, mean, scale, eps):
                nc.vector.tensor_scalar(small[:, 10:12], mean, scale, eps, ALU.mult, ALU.add).then_inc(ms_ready, 1)
                dve.wait_ge(root_ready, n)
                r0, t, r, a = small[:, 14:16], small[:, 16:18], small[:, 18:20], small[:, 10:12]
                link(nc.vector.reciprocal(r0, small[:, 12:14]))
                link(nc.vector.tensor_tensor(t, r0, r0, ALU.mult))
                link(nc.vector.tensor_tensor(t, t, a, ALU.mult))
                link(nc.vector.tensor_scalar(t, t, -0.5, 1.5, ALU.mult, ALU.add))
                link(nc.vector.tensor_tensor(r, r0, t, ALU.mult))

            def norm_scale(k):
                dve.wait_ge(sq_ready, 8 * (k + 1))
                link(nc.vector.tensor_reduce(small[:, 8:10], small[:, 0:8].rearrange("p (b c) -> p b c", b=2), AX.X, ALU.add))
                inverse_root(ROOT[k], small[:, 8:10], 1.0 / D, EPS_RMS)

            def norm_x(k):
                norm_scale(k)
                for ch in range(4):
                    for b in range(2):
                        cs = slice(ch * 512, (ch + 1) * 512)
                        nc.vector.tensor_scalar(nrm[:, b, cs], xs[:, b, cs], small[:, 18 + b:19 + b], None,
                                                ALU.mult).then_inc(n_ready, 1)

            def norm_mod(k, g_col, layer, part, units):
                dve.wait_ge(mod_ready, units)
                m0 = 96 * layer + 48 * part
                link(nc.vector.scalar_tensor_tensor(out=amul[:, :], in0=mod[:, m0 + 16:m0 + 32], scalar=1.0,
                                                    in1=cols[:, 0, g_col:g_col + 16], op0=ALU.add, op1=ALU.mult))

            def norm_lo(k, layer, part, q):
                m0 = 96 * layer + 48 * part
                for kt in range(4 * q, 4 * q + 4):
                    dve.wait_ge(nT_ready, 16 * k + 2 * (kt // 2) + 2)
                    if kt >= 4:
                        dve.wait_ge(hT_ready, 16 * k + kt - 3)
                    nc.vector.tensor_scalar(hid[:, kt % 4, :], ps[:, kt // 2, (kt % 2) * 256:(kt % 2 + 1) * 256],
                                            amul[:, kt:kt + 1], mod[:, m0 + kt:m0 + kt + 1], ALU.mult, ALU.add
                                            ).then_inc(h_ready, 1)
                for kt in range(4 * q, 4 * q + 4):
                    dve.wait_ge(hT_hi, 16 * k + kt + 1)
                    nc.vector.tensor_tensor(hTl[:, kt, :], hid[:, kt % 4, :], hTh[:, kt, :].bitcast(F32),
                                            ALU.subtract).then_inc(hT_ready, 1)

            def split_lo(step):
                for m in range(2):
                    dve.wait_ge(hid_hi, 2 * step + m + 1)
                    nc.vector.tensor_tensor(hidl[:, 2 * m:2 * m + 2, :], hid[:, 2 * m:2 * m + 2, :],
                                            hidh[:, 2 * m:2 * m + 2, :].bitcast(F32), ALU.subtract).then_inc(hid_lo, 1)

            def evac(n0, ch, units):
                dve.wait_ge(unit_done, units)
                for b in range(2):
                    k = 2 * ch + b
                    if not (isinstance(n0, int) and n0 + k < 2):
                        dve.wait_ge(x_added, n0 + k - 1)
                    nc.vector.tensor_tensor(tmp[:, b, :], ps[:, WD + k % 4, :], gate[:, ch * 512:(ch + 1) * 512],
                                            ALU.mult).then_inc(out_evac, 1)

            def diagonals(b, src):
                for ch in range(4):
                    if 4 * b + ch >= 2:
                        dve.wait_ge(bc_done, 4 * b + ch - 1)
                    for m in range(4):
                        ins = nc.vector.tensor_scalar(tmp[:, ch % 2, m * P:(m + 1) * P], ident[:, :],
                                                      src[:, 4 * ch + m:4 * ch + m + 1], None, ALU.mult)
                    ins.then_inc(diag_ready, 1)

            dve.wait_ge(table, 3)
            nc.vector.memset(wsT[64:128, :, 0:64], 0.0).then_inc(ws_ready, 1)
            dve.wait_ge(vec_landed, 16 * 14)
            link(nc.vector.tensor_scalar(negsink[:, :], negsink[:, :], -1.0, None, ALU.mult))
            link(nc.vector.tensor_copy(maskc[:, :], mask32))
            norm_x(0)

            dve.wait_ge(cond_ready, 1)
            dve.wait_ge(table, 2)

            def start_body(i):
                for e in range(8):
                    ada_group(S["start"], i, e, e, True)
                mod_add(2 * i, 0, 2 * i, 2, ADA_BANK["start"])
            start_body(0)
            with dve.Fori(1, 4) as i:
                start_body(i)
            norm_mod(0, MIXG, 0, 0, 8)

            def v_bias(t, slot, units):
                ch = 2 * t + slot
                dve.wait_ge(vb_landed[slot], 16 * t + 16)
                dve.wait_ge(unit_done, units)
                for b in range(2):
                    nc.vector.tensor_tensor(vT[:, bass.ds(4 * ch, 4), b, :],
                                            ps[:, 4 * slot + b, :].rearrange("p (t i) -> p t i", t=4),
                                            tmp[:, slot, :].rearrange("p (t i) -> p t i", t=4), ALU.add
                                            ).then_inc(v_biased, 1)

            def v_stat(ch):
                for b in range(2):
                    dve.wait_ge(v_gelu, 2 * ch + b + 1)
                    for_chunk = vT[:, bass.ds(4 * ch, 4), b, :]
                    nc.vector.bn_stats(vst[:, b, bass.ds(ch, 1), :].rearrange("p a s -> p (a s)"), for_chunk).then_inc(v_stats, 1)

            def v_hooks(t, units, first):
                def hooks(q):
                    if first and q < 4:
                        norm_lo(0, 0, 0, q)
                    if not first:
                        if q == 0:
                            v_bias(t - 1, 1, units)
                        if q == 1:
                            v_stat(2 * t - 1)
                    if q == 4:
                        v_bias(t, 0, units + 8)
                    if q == 5:
                        v_stat(2 * t)
                    if q == 6:
                        mod_add(t + 8, 0, t + 8, 1, ADA_BANK["v"])
                return hooks
            run(S["v0"], 0, v_hooks(0, S["v0"].unit(), True), False)
            with dve.Fori(0, 5) as i:
                run(S["v"], i, v_hooks(i + 1, S["v"].unit(i), False), False)

            def u_mul(j):
                for m in range(2):
                    dve.wait_ge(gelu_u, 2 * j + m + 1)
                    nc.vector.tensor_tensor(hid[:, 2 * m:2 * m + 2, :], hid[:, 2 * m:2 * m + 2, :],
                                            vT[:, bass.ds(4 * j + 2 * m, 2), :, :].rearrange("p t b i -> p t (b i)"),
                                            ALU.mult).then_inc(hid_ready, 1)

            def v_layer_norm():
                dve.wait_ge(v_stats, 2 * GM_STEPS)
                for b in range(2):
                    link(nc.vector.bn_aggr(small[:, 20 + 2 * b:22 + 2 * b], vst[:, b, :, :].rearrange("p a s -> p (a s)")))
                inverse_root(ROOT_LN, small[:, 21:24:2], 1.0, EPS_LN)

            def v_scale(b):
                for k in range(3):
                    part = vT[:, 16 * k:16 * k + 16, b, :]
                    nc.vector.tensor_scalar(part, part, small[:, 20 + 2 * b:21 + 2 * b], small[:, 18 + b:19 + b],
                                            ALU.subtract, ALU.mult).then_inc(v_normed, 1)

            def mix_out():
                dve.wait_ge(bs_landed, 16)
                dve.wait_ge(table, 4)
                for pr in range(ET // 2):
                    for m in range(2):
                        ti = 2 * pr + m
                        nc.vector.scalar_tensor_tensor(out=tmp[:, pr % 2, m * P:(m + 1) * P], in0=rs_bc[:, ti // TPG, :],
                                                       scalar=lnb[:, ti:ti + 1], in1=bs_bc[:, ti // TPG, :],
                                                       op0=ALU.mult, op1=ALU.add).then_inc(mix_t, 1)
                    dve.wait_ge(mix_done, pr + 1)
                    for m in range(2):
                        ti = 2 * pr + m
                        dve.wait_ge(mix_t, ti + 1)
                        nc.vector.scalar_tensor_tensor(
                            out=vT[:, ti, :, :], in0=ps[:, WD + pr % 4, m * 256:(m + 1) * 256].rearrange("p (b i) -> p b i", b=2),
                            scalar=lng[:, ti:ti + 1],
                            in1=tmp[:, pr % 2, m * P:(m + 1) * P].unsqueeze(1).to_broadcast([P, 2, P]),
                            op0=ALU.mult, op1=ALU.add).then_inc(mixed, 1)

            def u_pro_hooks(q):
                if q == 0:
                    v_bias(GM_STEPS // 2 - 1, 1, S["u_pro"].unit())
                if q == 1:
                    v_stat(GM_STEPS - 1)
                    v_layer_norm()
                if 2 <= q <= 3:
                    v_scale(q - 2)
                if q == 5:
                    mix_out()
                    u_mul(0)
                    split_lo(0)
            run(S["u_pro"], 0, u_pro_hooks, False)
            dve.wait_ge(mod_ready, 12)
            diagonals(0, mod[:, 32:48])

            def u_hooks(j, units):
                n0 = 8 * (j - 1)

                def hooks(q):
                    if q == 1:
                        dve.wait_ge(mixed, ET)
                        u_mul(j)
                    if 1 <= q <= 4:
                        evac(n0, q - 1, units + 2 * q)
                    if q == 4:
                        split_lo(j)
                    if q == 6:
                        mod_add(j + 13, 0, j + 13, 1, ADA_BANK["u"])
                return hooks
            run(S["u_first"], 0, u_hooks(1, S["u_first"].unit()), False)
            with dve.Fori(0, 9) as i:
                run(S["u"], i, u_hooks(i + 2, S["u"].unit(i)), False)
            L = GM_STEPS - 1

            def u_epi_hooks(q):
                if q == 1:
                    u_mul(L)
                if 1 <= q <= 4:
                    evac(8 * (L - 1), q - 1, S["u_epi"].unit() + 2 * q)
                if q == 4:
                    split_lo(L)
                if q >= 5:
                    evac(8 * L, q - 5, S["u_epi"].unit() + 2 * q)
            run(S["u_epi"], 0, u_epi_hooks, False)
            evac(8 * L, 3, S["u_epi"].unit() + 16)

            def ffn(l, tag, k_norm, g_b, ada_pro, ada_loop, ada_epi):
                s0, n0 = STEP_F[l], EV_F[l]

                def up_mul(j, units):
                    dve.wait_ge(unit_done, units)
                    for m in range(2):
                        dve.wait_ge(silu_g, 2 * (l * FF_STEPS + j) + m + 1)
                        half = hid[:, 2 * m:2 * m + 2, :].rearrange("p a c -> p (a c)")
                        nc.vector.tensor_tensor(half, half, ps[:, WU + m, :], ALU.mult).then_inc(hid_ready, 1)

                def pro_hooks(q):
                    if q == 0:
                        norm_x(k_norm)
                        norm_mod(k_norm, FFNG + 16 * l, l, 1, 24 * l + 20)
                    if q < 4:
                        norm_lo(k_norm, l, 1, q)
                    if q == 9:
                        up_mul(0, S[tag + "_pro"].unit() + 16)
                        split_lo(s0)
                    if q == 10:
                        mod_add(ada_pro, 1, ada_pro - 24, 2, ADA_BANK["ffn"])
                run(S[tag + "_pro"], 0, pro_hooks, True)
                dve.wait_ge(mod_ready, 24 * (l + 1))
                dve.wait_ge(x_added, n0)
                diagonals(g_b, mod[:, 96 * l + 80:96 * l + 96])

                def hooks_of(j, units, ada):
                    m0 = n0 + 8 * (j - 1)

                    def hooks(q):
                        if q == 5:
                            up_mul(j, units + 8)
                        if 5 <= q <= 8:
                            evac(m0, q - 5, units + 2 * q)
                        if q == 8:
                            split_lo(s0 + j)
                        if q == 10 and ada is not None:
                            mod_add(ada, 1, ada - 24, 2, ADA_BANK["ffn"])
                    return hooks
                with dve.Fori(0, 9) as i:
                    run(S[tag], i, hooks_of(i + 1, S[tag].unit(i), ada_loop(i)), True)
                J = FF_STEPS - 1

                def epi_hooks(q):
                    hooks_of(J, S[tag + "_epi"].unit(), ada_epi)(q)
                    if q >= 9:
                        evac(n0 + 8 * J, q - 9, S[tag + "_epi"].unit() + 2 * q)
                run(S[tag + "_epi"], 0, epi_hooks, True)
                evac(n0 + 8 * J, 3, S[tag + "_epi"].unit() + 24)

            ffn(0, "f0", 1, 1, 24, lambda i: 2 * i + 26, 44)

            def rope(pair):
                dst = (qT if pair < 8 else kT)[:, (2 * pair) % 16:(2 * pair) % 16 + 2, :]
                cosb = trig[:, 0, :].unsqueeze(1).to_broadcast([P, 2, 256])
                sinb = trig[:, 1, :].unsqueeze(1).to_broadcast([P, 2, 256])
                dve.wait_ge(rot_done, pair + 1)
                bank = WD + pair % 4
                link(nc.vector.tensor_tensor(rtmp, ps[:, bank, :].rearrange("p (t q) -> p t q", t=2), sinb, ALU.mult))
                link(nc.vector.tensor_tensor(dst, dst, cosb, ALU.mult))
                nc.vector.tensor_tensor(dst, dst, rtmp, ALU.add).then_inc(roped, 1)
                dve.wait_ge(roped, pair + 1)

            def qkv_hooks(q):
                if q == 0:
                    norm_x(2)
                    norm_mod(2, MIXG + 16, 1, 0, 32)
                    dve.wait_ge(att_landed, 48)
                if q < 4:
                    norm_lo(2, 1, 0, q)
                if q >= 5 and q % 4 == 1:
                    rope(2 * (q // 4 - 1))
                    rope(2 * (q // 4 - 1) + 1)
            run(S["qkv"], 0, qkv_hooks, False)
            dve.wait_ge(unit_done, S["qkv"].unit() + 40)
            nc.vector.tensor_tensor(vtok[:, :, :], ps[:, 1, :].rearrange("p (b d) -> p b d", b=2),
                                    vb_bc.unsqueeze(1).to_broadcast([P, 2, 256]), ALU.add).then_inc(vtok_ready, 1)
            rope(8)

            def quad_max(Q):
                s, bk = Q % 2, 3 * (Q % 2)
                for k, r in enumerate((1, 2, 0)):
                    dve.wait_ge(s_done, 3 * Q + k + 1)
                    dst, src = (stat[:, 0, s, 0:4], ps[:, bk, :].rearrange("p (h k) -> p h k", h=4)) if r == 0 else \
                        (stat[:, 0, s, 3 + r:8:2], ps[:, bk + r, :].rearrange("p (h k) -> p h k", h=2))
                    ins = nc.vector.tensor_reduce(dst, src, AX.X, ALU.max)
                    link(ins)
                ns = negsink[:, 4 * Q:4 * Q + 4].unsqueeze(1).to_broadcast([P, 2, 4])
                two = lambda k: stat[:, k, s, :].rearrange("p (m h) -> p m h", m=2)
                nc.vector.scalar_tensor_tensor(out=two(1), in0=two(0), scalar=-0.125, in1=ns,
                                               op0=ALU.mult, op1=ALU.min).then_inc(s_max, 1)
                dve.wait_ge(s_max, 2 * Q + 1)
                nc.vector.tensor_tensor(two(2), two(1), ns, ALU.subtract).then_inc(s_max, 1)

            def quad_norm(Q):
                s = Q % 2
                dve.wait_ge(p_exp, 9 * (Q + 1))
                link(nc.vector.tensor_tensor(stat[:, 5, s, :], stat[:, 3, s, :], stat[:, 4, s, :], ALU.add))
                link(nc.vector.reciprocal(stat[:, 6, s, :], stat[:, 5, s, :]))
                for i in range(8):
                    mb, r = i // 4, i % 4
                    pp = prob[:, s, r * 128:(r + 1) * 128] if mb == 0 else prob[:, s, 512 + r * 256:512 + (r + 1) * 256]
                    nc.vector.tensor_scalar(pp, pp, stat[:, 6, s, i:i + 1], None, ALU.mult).then_inc(p_norm, 1)

            def quad_out(Q):
                bk = 3 * (Q % 2)
                if Q >= 1:
                    dve.wait_ge(o_done, Q)
                dve.wait_ge(pt_done, 3 * Q + 1)
                nc.vector.tensor_copy(probT[:, 0], ps[:, bk, :].rearrange("p (h q) -> p h q", h=4)).then_inc(pt_v, 1)
                dve.wait_ge(o_hi, Q + 1)
                nc.vector.tensor_tensor(hTl[:, 2 * Q:2 * Q + 2, :], ps[:, 6 + Q % 2, :].rearrange("p (t q) -> p t q", t=2),
                                        hTh[:, 2 * Q:2 * Q + 2, :].bitcast(F32), ALU.subtract).then_inc(o_lo, 1)
            NQD = NQ // 4
            quad_max(0)
            for Q in range(NQD):
                if Q + 1 < NQD:
                    quad_max(Q + 1)
                quad_norm(Q)
                quad_out(Q)
            dve.wait_ge(mod_ready, 36)
            diagonals(2, mod[:, 96 + 32:96 + 48])
            gb = small[:, 32:48]
            link(nc.vector.tensor_tensor(gb, mod[:, 96 + 32:96 + 48], cols[:, 0, BO:BO + 16], ALU.mult))
            diagonals(3, gb)
            for ch in range(4):
                dve.wait_ge(bc_done, 12 + ch + 1)
                for b in range(2):
                    xc = xs[:, b, ch * 512:(ch + 1) * 512]
                    nc.vector.tensor_tensor(xc, xc, ps[:, ch, :], ALU.add).then_inc(bo_added, 1)
            dve.wait_ge(gate_evac, 12)

            def wo_hooks(q):
                if q >= 4 and q % 4 == 0:
                    evac(EV_WO, q // 4 - 1, S["wo"].unit() + 2 * q)
            run(S["wo"], 0, wo_hooks, False)
            evac(EV_WO, 3, S["wo"].unit() + 32)
            ffn(1, "f1", 3, 4, 46, lambda i: None, None)

            dve.wait_ge(fg_landed, 16)
            norm_scale(4)
            for b in range(2):
                nc.vector.scalar_tensor_tensor(out=outs[:, b, :], in0=xs[:, b, :], scalar=small[:, 18 + b:19 + b],
                                               in1=fg_bc, op0=ALU.mult, op1=ALU.mult).then_inc(out_ready, 1)

        @block.tensor
        def _(pe):
            mm = nc.tensor.matmul

            pe.wait_ge(vec_landed, 16 * 14)
            nc.tensor.transpose(ps[:, 6, 0:P], nat[:, 0, :], ident[:, :]).then_inc(turned, 1)
            for t in range(1, 5):
                ins = nc.tensor.transpose(ps[:, 5, (t - 1) * P:t * P], nat[:, t, :], ident[:, :])
            ins.then_inc(turned, 1)
            for g in range(GROUPS):
                ins = nc.tensor.transpose(ps[:, 3 + g // 4, (g % 4) * P:(g % 4 + 1) * P], wsn[:, g, :], ident[:, :])
            ins.then_inc(turned, 1)
            pe.wait_ge(ws_ready, 1)
            pe.wait_ge(ones_ready, 1)
            for m in range(2):
                ins = mm(ps[:, 1 + m, :], ones[:, :], wsT[:, 4 * m:4 * m + 4, :].rearrange("p g i -> p (g i)"), start=True, stop=True)
            ins.then_inc(turned, 1)

            def ada_reduce(piece, i, units, bank):
                e = piece.pos[("A", 4 * units - 1)]
                pe.wait_ge(raw_used, 16 * piece.turn(i) + 4 * e + 4)
                for k in range(4 * units):
                    ins = mm(ps[:, bank, k:k + 1], acc[:, k // 4, (k % 4) * P:(k % 4 + 1) * P], ones[:, 0:1],
                             start=True, stop=True)
                    if k % 4 == 3:
                        ins.then_inc(ada_reduced, 1)

            def staged(piece, i, q, h):
                pe.wait_ge(raw_used, 16 * piece.turn(i) + 4 * piece.pos[("W", q)] + 2 * h + 2)
                return (2 * q + h) % 4

            def finish_unit(ins):
                ins.then_inc(unit_done, 1)

            def feature_major(piece, i, q0, bank, h_base=None, tiles=4, ahead=None):
                for g in range(4):
                    if ahead is not None:
                        ahead(q0 + g)
                    for h in range(2):
                        s = staged(piece, i, q0 + g, h)
                        for kk in range(2):
                            kt = 4 * g + 2 * h + kk
                            if h_base is not None:
                                pe.wait_ge(hT_ready, h_base + max(kt + 1, 4))
                            for m in range(tiles):
                                o = ps[:, bank + m // 2, (m % 2) * 256:(m % 2 + 1) * 256]
                                a = slice(m * P, (m + 1) * P)
                                mm(o, whi[:, s, kk, a], hTh[:, kt, :], start=(kt == 0 and m % 2 == 0), stop=False)
                                mm(o, whi[:, s, kk, a], hTl[:, kt, :], start=False, stop=False)
                                ins = mm(o, wlo[:, s, kk, a], hTh[:, kt, :], start=False,
                                         stop=(kt == KD - 1 and m % 2 == 1))
                            if tiles == 2:
                                for b in range(2):
                                    o, a = ps[:, bank + 1, b * 256:(b + 1) * 256], slice(b * P, (b + 1) * P)
                                    mm(o, hTh[:, kt, a], whi[:, s, kk, 256:512], start=(kt == 0 and b == 0), stop=False)
                                    mm(o, hTh[:, kt, a], wlo[:, s, kk, 256:512], start=False, stop=False)
                                    ins = mm(o, hTl[:, kt, a], whi[:, s, kk, 256:512], start=False,
                                             stop=(kt == KD - 1 and b == 1))
                        finish_unit(ins)

            def token_major(piece, i, q0, groups, lh, ll, banks, free=None, h_base=None, ahead=None):
                for g in range(groups):
                    if ahead is not None:
                        ahead(q0 + g)
                    for h in range(2):
                        s = staged(piece, i, q0 + g, h)
                        for b in range(2):
                            if g == 0 and h == 0 and free is not None:
                                free(b)
                            for kk in range(2):
                                kt = 4 * g + 2 * h + kk
                                if h_base is not None and b == 0:
                                    pe.wait_ge(hT_ready, h_base + max(kt + 1, 4))
                                o, a = ps[:, banks + b, :], slice(b * P, (b + 1) * P)
                                mm(o, lh[:, kt, a], whi[:, s, kk, :], start=(kt == 0), stop=False)
                                mm(o, lh[:, kt, a], wlo[:, s, kk, :], start=False, stop=False)
                                ins = mm(o, ll[:, kt, a], whi[:, s, kk, :], start=False, stop=(kt == 4 * groups - 1))
                        finish_unit(ins)

            def turn_x(k):
                for kt in range(KD):
                    pe.wait_ge(n_ready, 8 * k + 2 * (kt // 4) + 2)
                    for b in range(2):
                        ins = nc.tensor.transpose(ps[:, kt // 2, (kt % 2) * 256 + b * P:(kt % 2) * 256 + (b + 1) * P],
                                                  nrm[:, b, kt * P:(kt + 1) * P], ident[:, :])
                    ins.then_inc(nT_ready, 1)

            def output_chunk(piece, i, q, n0, ch, groups=1, lh=hidh, ll=hidl):
                def free(b):
                    n = n0 + 2 * ch + b
                    if not (isinstance(n, int) and n < 4):
                        pe.wait_ge(out_evac, n - 3)
                token_major(piece, i, q, groups, lh, ll, WD + 2 * (ch % 2), free)

            def rows_of(b, bank):
                for ch in range(4):
                    pe.wait_ge(diag_ready, 4 * b + ch + 1)
                    mm(ps[:, bank + ch, :], ones[:, :], tmp[:, ch % 2, :], start=True, stop=True).then_inc(bc_done, 1)

            pe.wait_ge(table, 4)

            def start_body(i):
                for k in range(2):
                    pe.wait_ge(raw_used, 32 * i + 16 * k + 16)
                    if not isinstance(i, int):
                        pe.wait_ge(mod_ready, 2 * i)
                    for m in range(4):
                        ins = mm(ps[:, ADA_BANK["start"], 4 * k + m:4 * k + m + 1], acc[:, k, m * P:(m + 1) * P],
                                 ones[:, 0:1], start=True, stop=True)
                    ins.then_inc(ada_reduced, 1)
            start_body(0)
            with pe.Fori(1, 4) as i:
                start_body(i)
            pe.wait_ge(mod_ready, 8)
            turn_x(0)

            def v_body(piece, i, t):
                first = isinstance(t, int)

                def ahead(q):
                    if q == 6:
                        if not first:
                            pe.wait_ge(mod_ready, t + 8)
                        ada_reduce(piece, i, 1, ADA_BANK["v"])
                if not first:
                    pe.wait_ge(v_biased, 4 * t - 2)
                token_major(piece, i, 0, 4, hTh, hTl, 0, h_base=0 if first else None)
                if not first:
                    pe.wait_ge(v_biased, 4 * t)
                token_major(piece, i, 4, 4, hTh, hTl, 4, ahead=ahead)
            v_body(S["v0"], 0, 0)
            with pe.Fori(0, 5) as i:
                v_body(S["v"], i, i + 1)

            feature_major(S["u_pro"], 0, 0, WU)
            pe.wait_ge(v_biased, 2 * GM_STEPS)
            pe.wait_ge(v_normed, 6)
            for pr in range(ET // 2):
                if pr >= 4:
                    pe.wait_ge(mixed, 2 * (pr - 3))
                for m in range(2):
                    ti = 2 * pr + m
                    for b in range(2):
                        ins = mm(ps[:, WD + pr % 4, m * 256 + b * P:m * 256 + (b + 1) * P], vT[:, ti, b, :],
                                 wsT[:, ti // TPG, :], start=True, stop=True)
                ins.then_inc(mix_done, 1)
            pe.wait_ge(gelu_u, 2)
            feature_major(S["u_pro"], 0, 4, WU)
            rows_of(0, WD)
            pe.wait_ge(gate_evac, 4)

            def u_body(piece, i, j):
                pe.wait_ge(hid_lo, 2 * j)
                for ch in range(4):
                    output_chunk(piece, i, ch, 8 * (j - 1), ch)

                def ahead(q):
                    if q == 6:
                        if not isinstance(j, int):
                            pe.wait_ge(mod_ready, j + 13)
                        ada_reduce(piece, i, 1, ADA_BANK["u"])
                pe.wait_ge(gelu_u, 2 * j + 2)
                feature_major(piece, i, 4, WU, ahead=ahead)
            u_body(S["u_first"], 0, 1)
            with pe.Fori(0, 9) as i:
                u_body(S["u"], i, i + 2)
            for k in range(2):
                pe.wait_ge(hid_lo, 2 * (GM_STEPS - 1 + k))
                for ch in range(4):
                    output_chunk(S["u_epi"], 0, 4 * k + ch, 8 * (GM_STEPS - 2 + k), ch)

            def ffn(l, tag, k_norm, row):
                s0, n0, g0 = STEP_F[l], EV_F[l], 2 * l * FF_STEPS
                turn_x(k_norm)

                def reduce_at(piece, i, s, ada):
                    def ahead(q):
                        if q == 10:
                            pe.wait_ge(hid_ready, 2 * s + 2)
                            ada_reduce(piece, i, 2, ADA_BANK["ffn"])
                    return ahead if ada is not None else None
                pro, epi = S[tag + "_pro"], S[tag + "_epi"]
                ada0, ada_l, ada_e = ((24, lambda i: 2 * i + 26, 44), (46, lambda i: None, None))[l]
                feature_major(pro, 0, 0, WG, h_base=16 * k_norm)
                feature_major(pro, 0, 4, WU)
                pe.wait_ge(silu_g, g0 + 2)
                feature_major(pro, 0, 8, WG, ahead=reduce_at(pro, 0, s0, ada0))
                rows_of(row, WD)
                pe.wait_ge(gate_evac, (8, 16)[l])

                def body(piece, i, j, ada):
                    if ada is not None or l == 0:
                        pe.wait_ge(mod_ready, ada)
                    pe.wait_ge(hid_ready, 2 * (s0 + j))
                    feature_major(piece, i, 0, WU)
                    pe.wait_ge(hid_lo, 2 * (s0 + j))
                    for ch in range(4):
                        output_chunk(piece, i, 4 + ch, n0 + 8 * (j - 1), ch)
                with pe.Fori(0, 9) as i:
                    j = i + 1
                    body(S[tag], i, j, ada_l(i))
                    pe.wait_ge(silu_g, g0 + 2 * j + 2)
                    feature_major(S[tag], i, 8, WG, ahead=reduce_at(S[tag], i, s0 + j, ada_l(i)))
                body(epi, 0, FF_STEPS - 1, ada_e)
                pe.wait_ge(hid_lo, 2 * (s0 + FF_STEPS))
                last = reduce_at(epi, 0, s0 + FF_STEPS - 1, ada_e)
                for ch in range(4):
                    if last is not None:
                        last(8 + ch)
                    output_chunk(epi, 0, 8 + ch, n0 + 8 * (FF_STEPS - 1), ch)
            ffn(0, "f0", 1, 1)

            turn_x(2)

            def rotated(pair):
                pe.wait_ge(q_bias, pair + 1)
                if pair >= 4:
                    pe.wait_ge(roped, pair - 3)
                src = (qT if pair < 8 else kT)[:, (2 * pair) % 16:(2 * pair) % 16 + 2, :]
                mm(ps[:, WD + pair % 4, :], rot, src.rearrange("p t q -> p (t q)"), start=True, stop=True).then_inc(rot_done, 1)

            def rotate_chunk(ch):
                def ahead(q):
                    if q == 4 * ch + 1 and ch >= 1:
                        if ch == 1:
                            pe.wait_ge(att_landed, 48)
                        rotated(2 * ch - 2)
                        rotated(2 * ch - 1)
                return ahead
            for ch in range(5):
                if ch >= 2:
                    pe.wait_ge(q_bias, 2 * ch - 2)
                feature_major(S["qkv"], 0, 4 * ch, 2 * (ch % 2), h_base=32 if ch == 0 else None,
                              tiles=2 if ch == 4 else 4, ahead=rotate_chunk(ch))
            rotated(8)
            pe.wait_ge(roped, 9)
            for g in range(4):
                for half in range(2):
                    ins = mm(ps[64 * half:64 * half + 64, 6 + g // 2, (g % 2) * 256:(g % 2 + 1) * 256],
                             ident[:, (g % 2) * 64:(g % 2) * 64 + 64], kT[:, g // 2, :], start=True, stop=True)
                if g % 2:
                    ins.then_inc(dup_done, 1)

            def scores(Q):
                bk, g = 3 * (Q % 2), Q // 2
                if Q >= 2:
                    pe.wait_ge(pt_v, Q - 1)
                    pe.wait_ge(pt_a, 2 * (Q - 1))
                for r in range(3):
                    mrow, n = (maskc[:, 128:256], 4) if r == 0 else (maskc[:, 256:512], 2)
                    mm(ps[:, bk + r, :].rearrange("p (h k) -> p h k", h=n), maskc[:, 0:128],
                       mrow.unsqueeze(1).to_broadcast([2, n, 512 // n]), start=True, stop=False)

                def head(hh, block):
                    half = slice(64 * (hh % 2), 64 * (hh % 2) + 64)
                    o = ps[:, bk, hh * 128:hh * 128 + 128] if block == 0 else \
                        ps[:, bk + 1 + hh % 2, (hh // 2) * 256:(hh // 2) * 256 + 256]
                    return mm(o, qT[half, 2 * Q + hh // 2, block * P:(block + 1) * P], kdup[half, g, 0:P * (block + 1)],
                              start=False, stop=(hh == 3 if block == 0 else hh >= 2))
                head(0, 0)
                head(2, 0).then_inc(s_even, 1)
                for hh in (0, 2, 1, 3):
                    ins = head(hh, 1)
                    if hh >= 2:
                        ins.then_inc(s_done, 1)
                pe.wait_ge(s_even, Q + 1)
                head(1, 0)
                head(3, 0).then_inc(s_done, 1)

            def attend(Q):
                bk, s, g = 3 * (Q % 2), Q % 2, Q // 2
                pe.wait_ge(p_norm, 8 * (Q + 1))
                for r in range(3):
                    for b in range(4):
                        col = b * P if r == 0 else 512 + (2 * (r - 1) + b // 2) * 256 + (b % 2) * P
                        ins = nc.tensor.transpose(ps[:, bk + r, b * P:(b + 1) * P], prob[:, s, col:col + P], ident[:, :])
                    ins.then_inc(pt_done, 1)
                pe.wait_ge(pt_v, Q + 1)
                pe.wait_ge(pt_a, 2 * (Q + 1))
                if Q >= 2:
                    pe.wait_ge(o_lo, Q - 1)
                for hh in range(4):
                    vcol = slice(g * 64, g * 64 + 64)
                    for mb in range(2):
                        o = ps[64 * (hh % 2):64 * (hh % 2) + 64, 6 + s, (hh // 2) * 256 + mb * P:(hh // 2) * 256 + (mb + 1) * P]
                        for kb in range(mb + 1):
                            pt = probT[:, 0, hh, :] if mb == 0 else probT[:, 1 + hh // 2, 2 * (hh % 2) + kb, :]
                            ins = mm(o, vtok[:, kb, vcol], pt, start=(hh < 2 and mb == 0),
                                     stop=(hh >= 2 and mb == 1 and kb == 1))
                ins.then_inc(o_done, 1)
            pe.wait_ge(dup_ready, 2)
            pe.wait_ge(vtok_ready, 1)
            NQD = NQ // 4
            scores(0)
            for Q in range(NQD):
                if Q + 1 < NQD:
                    scores(Q + 1)
                attend(Q)
            pe.wait_ge(o_lo, NQD)
            rows_of(2, WD)
            rows_of(3, 0)
            pe.wait_ge(gate_evac, 12)
            for ch in range(4):
                output_chunk(S["wo"], 0, 4 * ch, EV_WO, ch, groups=4, lh=hTh, ll=hTl)
            ffn(1, "f1", 3, 4)


_INS = ["x", "c", "ada_w", "ada_b", "mix_norm_g", "ffn_norm_g", "gm_w_in", "gm_b_in", "gm_ln_g", "gm_ln_b", "gm_w_s",
        "gm_b_s", "gm_w_out", "sw_w_qkv", "sw_b_qkv", "sw_sinks", "sw_w_o", "sw_b_o", "ffn_w_gu", "ffn_w_down", "final_g"]


def _constants():
    import numpy as np

    f = np.float32
    ident = np.eye(128, dtype=f)
    rot = np.zeros((128, 128), f)
    for m in range(128):
        rot[m + 32 if m % 64 < 32 else m - 32, m] = -1.0 if m % 64 < 32 else 1.0
    inv = (f(1.0) / (f(10000.0) ** (np.arange(0, 64, 2, dtype=f) / f(64.0)))).astype(f)
    ang = (np.arange(256, dtype=f)[None, :] * inv[np.arange(128) % 32][:, None]).astype(f)
    a = np.concatenate([ident, rot, np.cos(ang), np.sin(ang)], 1).astype(f)
    mask = np.zeros((2, 512), f)
    mask[0, 0:64], mask[1, 64:128] = 1.0, 1.0
    mask[0, 128 + 64:256] = -1e30
    mask[0, 256:256 + 64], mask[0, 256 + 192:512] = -1e30, -1e30
    mask[1, 256:256 + 128] = -1e30
    return a, mask


def kernel(**inputs):
    import numpy as _np
    import concourse.bacc as _bacc
    from concourse import mybir as _mybir
    from concourse.bass_utils import run_bass_kernel_spmd as _run

    nc = _bacc.Bacc("TRN2", target_bir_lowering=False, num_devices=1)
    consts, mask = _constants()
    arrays, args = {}, []
    for name, a in [(n, inputs[n]) for n in _INS] + [("consts", consts), ("mask", mask)]:
        a = _np.ascontiguousarray(a)
        arrays[f"in_{name}_dram"] = a
        args.append(nc.dram_tensor(f"in_{name}_dram", a.shape, _mybir.dt.from_np(a.dtype), kind="ExternalInput").ap())
    shape = (1, 256, 2048)
    args.append(nc.dram_tensor("out_0_dram", shape, _mybir.dt.float32, kind="ExternalOutput").ap())
    trunk(nc, *args)
    r = _run(nc, [arrays], core_ids=[0])
    return r.results[0]["out_0_dram"]
```

```python
from contextlib import ExitStack

import concourse.bass as bass
from concourse import mybir

F32 = mybir.dt.float32
F32R = mybir.dt.float32r
BF16 = mybir.dt.bfloat16
ALU = mybir.AluOpType
ACT = mybir.ActivationFunctionType
AX = mybir.AxisListType

P = 128
WG, WU, WD = 0, 2, 4
ADA_BANK = {"start": 7, "v": 7, "u": 0, "ffn": 2}
EPS_RMS, EPS_LN = 1e-6, 1e-5


def w_order(n_w, n_ada, q0):
    after = [q0 + int((k + 0.5) * (n_w - 2 - q0) / n_ada) for k in range(n_ada)] if n_w else []
    order = [] if n_w else [("A", k) for k in range(n_ada)]
    for q in range(n_w):
        order.append(("W", q))
        order += [("A", k) for k in range(n_ada) if after[k] == q]
    return order


class Piece:

    def __init__(self, n_w, n_ada, turn, unit, red, reps=1, q0=0):
        self.order = w_order(n_w, n_ada, q0)
        self.n_w, self.n_ada, self.reps = n_w, n_ada, reps
        self.n_red = -(-n_ada // 8)
        self.turn0, self.unit0, self.red0 = turn, unit, red
        self.pos = {k: e for e, k in enumerate(self.order)}

    def turn(self, i=0):
        return self.turn0 + i * (len(self.order) // 4)

    def unit(self, i=0):
        return self.unit0 + i * (2 * self.n_w)

    def red(self, i=0):
        return self.red0 + i * self.n_red

    def after(self):
        return self.turn(self.reps), self.unit(self.reps), self.red(self.reps)


def trunk(nc, x, c, ada_w, ada_b, mix_norm_g, ffn_norm_g, gm_w_in, gm_b_in, gm_ln_g, gm_ln_b, gm_w_s,
          gm_b_s, gm_w_out, sw_w_qkv, sw_b_qkv, sw_sinks, sw_w_o, sw_b_o, ffn_w_gu, ffn_w_down, final_g,
          consts, mask_consts, out):
    D = x.shape[2]
    KD = D // P
    E = gm_w_out.shape[1]
    FF = ffn_w_down.shape[1]
    GM_STEPS, FF_STEPS = E // 512, FF // 512
    ET = E // P
    GROUPS = gm_w_s.shape[1]
    TPG = ET // GROUPS
    NQ = sw_sinks.shape[1]
    ATT = NQ * 64
    KV = (sw_w_qkv.shape[2] - ATT) // 2
    assert D == 2048 and x.shape[1] == 256 and KV == 256 and ATT == 2048 and GM_STEPS == 12 and FF_STEPS == 11

    at = (0, 0, 0)
    pieces = {}
    for name, n_w, n_ada, reps in (
            ("start", 0, 32, 1), ("v_first", 16, 8, 1), ("v", 16, 8, 2), ("u_pro", 8, 0, 1),
            ("u_first", 16, 8, 1), ("u", 16, 8, 4), ("u_epi", 8, 0, 1),
            ("f0_pro", 12, 8, 1), ("f0", 24, 8, 4), ("f0_epi", 24, 16, 1),
            ("qkv", 20, 16, 1), ("attend", 0, 16, 1), ("wo", 16, 8, 1),
            ("f1_pro", 12, 0, 1), ("f1", 24, 0, 4), ("f1_epi", 24, 0, 1)):
        q0 = 3 if name in ("v_first", "f0_pro", "qkv") else 2 if name == "wo" else 0
        pieces[name] = Piece(n_w, n_ada, *at, reps=reps, q0=q0)
        at = pieces[name].after()
    S = pieces
    SHIFT = (0, 48, 96, 144)
    RED_NORM = (4, 12, 19, 24)
    RED_GATE = (7, 12, 19, 24)
    STEP_F = (GM_STEPS, GM_STEPS + FF_STEPS)
    EV_F = (8 * GM_STEPS, 8 * (GM_STEPS + FF_STEPS) + 8)
    EV_WO = 8 * (GM_STEPS + FF_STEPS)
    EV_END = EV_F[1] + 8 * FF_STEPS

    def rot_bank(n):
        return 6 if n == 8 else WD + n % 4

    ROOT, ROOT_LN = (1, 3, 4, 5, 6), 2

    with ExitStack() as ctx:
        def sb(name, shape, dt):
            return ctx.enter_context(nc.sbuf_tensor(name, shape, dt))

        def sem(name):
            return ctx.enter_context(nc.semaphore(name))

        xs = sb("xs", [P, 2, D], F32)
        hTh = sb("hTh", [P, KD, 256], F32R)
        hTl = sb("hTl", [P, KD, 256], F32R)
        big = sb("big", [P, ET * 256], F32)
        hidh = sb("hidh", [P, 4, 256], F32R)
        hidl = sb("hidl", [P, 4, 256], F32R)
        hid = sb("hid", [P, 4, 256], F32)
        raw = sb("raw", [P, 4, 4, 512], F32)
        whi = sb("whi", [P, 4, 2, 512], F32R)
        wlo = sb("wlo", [P, 4, 2, 512], F32R)
        gate = sb("gate", [P, D], F32)
        rs_bc = gate[:, 0:GROUPS * P].rearrange("p (g i) -> p g i", g=GROUPS)
        bs_bc = gate[:, D - GROUPS * P:].rearrange("p (g i) -> p g i", g=GROUPS)
        acc = sb("acc", [P, 2, 1024], F32)
        tmp = sb("tmp", [P, 2, 512], F32)
        ident = sb("ident", [P, P], F32)
        ones = sb("ones", [P, P], F32)
        wsT = sb("wsT", [P, GROUPS, P], F32)
        cols = sb("cols", [P, 5, P], F32)
        mod = sb("mod", [P, 2 * 96], F32)
        rdiag = sb("rdiag", [P, 256], F32)[:, :]
        rrow = sb("rrow", [P, 256], F32)[:, :]
        ccol = sb("ccol", [P, KD], F32)
        amul = sb("amul", [P, KD], F32)
        small = sb("small", [P, 64], F32)
        vst = sb("vst", [P, 2, GM_STEPS, 6], F32)
        negsink = sb("negsink", [P, NQ], F32)
        stat = sb("stat", [P, 7, 2, 8], F32)
        maskc = sb("maskc", [2, 512], BF16)
        ps = ctx.enter_context(nc.psum_tensor("ps", [P, 8, 512], F32))

        raw_ada = raw[:, :, :, :].rearrange("p s k n -> p s (k n)").rearrange("p s (k n) -> p s k n", k=2)
        vT = big[:, :].rearrange("p (c b i) -> p c b i", b=2, i=P)
        nat = big[:, 4096:4736].rearrange("p (t i) -> p t i", t=5)
        wsn = big[:, 5120:6144].rearrange("p (g j) -> p g j", g=GROUPS)
        qT = big[:, 0:4096].rearrange("p (t q) -> p t q", t=16)
        kT = big[:, 4096:4608].rearrange("p (t q) -> p t q", t=2)
        kdup = big[:, 4608:5632].rearrange("p (g q) -> p g q", g=4)
        vtok = big[:, 5632:6144].rearrange("p (b d) -> p b d", b=2)
        prob = big[:, 6144:9216].rearrange("p (s n) -> p s n", s=2)
        probT = big[:, 9216:10752].rearrange("p (r h q) -> p r h q", r=3, h=4)
        trig = big[:, 10752:11264].rearrange("p (t q) -> p t q", t=2)
        rot = big[:, 11264:11392]
        vb_bc = big[:, 11392:11648]
        sin_part = [hid[:, 2 * m:2 * m + 2, :] for m in range(2)]
        outs = big[:, 4096:8192].rearrange("p (b d) -> p b d", b=2)
        bo_bc = big[:, 0:D]
        fg_bc = big[:, 8192:8192 + D]

        mask32 = big[0:2, 6144:6656]
        crow = big[0:16, 6656:6784]

        MIXG, FFNG, BQKV = 16, 48, 80
        adab = cols[:, 1:3, 0:96]
        bu, lng, lnb = cols[:, 3, 0:48], cols[:, 3, 48:96], cols[:, 4, 0:48]

        terms = tmp[:, :, :].rearrange("p s (h m i) -> p (s h) m i", h=2, m=2)

        raw_landed = [sem(f"raw_landed{i}") for i in range(4)]
        raw_used = sem("raw_used")
        hi_ready = sem("hi_ready")
        unit_done = sem("unit_done")
        ada_reduced = sem("ada_reduced")
        mod_ready = sem("mod_ready")
        vec_landed = sem("vec_landed")
        x_landed = sem("x_landed")
        bs_landed = sem("bs_landed")
        c_landed = sem("c_landed")
        c_turned = sem("c_turned")
        nat_zero = sem("nat_zero")
        ones_ready = sem("ones_ready")
        turned = sem("turned")
        table = sem("table")
        cond_ready = sem("cond_ready")
        ws_ready = sem("ws_ready")
        sq_ready = sem("sq_ready")
        ms_ready = sem("ms_ready")
        root_ready = sem("root_ready")
        rdiag_ready = sem("rdiag_ready")
        rrow_done = sem("rrow_done")
        rrow_taken = sem("rrow_taken")
        nT_ready = sem("nT_ready")
        h_ready = sem("h_ready")
        hT_hi = sem("hT_hi")
        hT_ready = sem("hT_ready")
        vb_landed = [sem(f"vb_landed{i}") for i in range(2)]
        v_biased = sem("v_biased")
        v_gelu = sem("v_gelu")
        v_stats = sem("v_stats")
        v_normed = sem("v_normed")
        mix_done = sem("mix_done")
        mix_rs = sem("mix_rs")
        mix_t = sem("mix_t")
        v_normed_b1 = sem("v_normed_b1")
        ln_ready = sem("ln_ready")
        bo_landed = sem("bo_landed")
        bo_gated = sem("bo_gated")
        mixed = sem("mixed")
        gelu_u = sem("gelu_u")
        silu_g = sem("silu_g")
        hid_ready = sem("hid_ready")
        hid_hi = sem("hid_hi")
        hid_lo = sem("hid_lo")
        out_evac = sem("out_evac")
        x_added = sem("x_added")
        diag_ready = sem("diag_ready")
        bc_done = sem("bc_done")
        gate_evac = sem("gate_evac")
        bo_added = sem("bo_added")
        dve_step = sem("dve_step")
        att_landed = sem("att_landed")
        q_bias = sem("q_bias")
        rot_done = sem("rot_done")
        rot_sin = sem("rot_sin")
        rot_cos = sem("rot_cos")
        roped = sem("roped")
        dup_done = sem("dup_done")
        dup_ready = sem("dup_ready")
        vtok_ready = sem("vtok_ready")
        s_done = sem("s_done")
        s_even = sem("s_even")
        s_max = sem("s_max")
        p_exp = sem("p_exp")
        p_norm = sem("p_norm")
        pt_done = sem("pt_done")
        pt_a = sem("pt_a")
        pt_v = sem("pt_v")
        o_done = sem("o_done")
        o_hi = sem("o_hi")
        o_lo = sem("o_lo")
        fg_landed = sem("fg_landed")
        out_ready = sem("out_ready")
        stored = sem("stored")

        block = ctx.enter_context(nc.Block())

        w_in, w_out = gm_w_in[0], gm_w_out[0]
        w_qkv, w_o = sw_w_qkv[0], sw_w_o[0]

        def tile_of(w, rows, col):
            return w[bass.ds(rows, 512), bass.ds(col, 512)].rearrange("(k p) n -> p k n", p=P)

        @block.sync
        def _(sp):
            def load(piece, i, q_src, ada_src):
                for e, (kind, q) in enumerate(piece.order):
                    turn = piece.turn(i)
                    if not (isinstance(turn, int) and 4 * turn + e < 4):
                        sp.wait_ge(raw_used, 16 * turn + 4 * e - 12)
                    src = q_src(q) if kind == "W" else ada_src(q)
                    dst = raw[:, e % 4] if kind == "W" else raw_ada[:, e % 4]
                    sp.dma_start(dst, src).then_inc(raw_landed[e % 4], 16)

            def ada_at(layer, unit):
                return lambda k: ada_w[layer][bass.ds(256 * (k % 8), 256),
                                              bass.ds((unit + k // 8) * 1024, 1024)].rearrange("(k p) n -> p k n", p=P)

            def v_src(i):
                return lambda q: tile_of(w_in, 512 * (q % 4), E + (4 * i + q // 4) * 512)

            def u_grp(j, q):
                return tile_of(w_in, 512 * q, j * 512)

            def out_grp(w, j, q):
                return tile_of(w, j * 512, 512 * q)

            def gate_grp(l, j, q):
                return tile_of(ffn_w_gu[l], 512 * q, j * 512)

            def up_grp(l, j, q):
                return tile_of(ffn_w_gu[l], 512 * q, FF + j * 512)

            load(S["start"], 0, None, ada_at(0, 0))
            load(S["v_first"], 0, v_src(0), ada_at(0, 4))
            with sp.Fori(0, 2) as i:
                load(S["v"], i, v_src(i + 1), ada_at(0, i + 5))
            load(S["u_pro"], 0, lambda q: u_grp(q // 4, q % 4), None)

            def u_src(j):
                return lambda q: out_grp(w_out, j - 1 + q // 8, q % 8) if q % 8 < 4 else \
                    u_grp(j + 1 + q // 8, q % 8 - 4)
            load(S["u_first"], 0, u_src(1), ada_at(0, 7))
            with sp.Fori(0, 4) as i:
                load(S["u"], i, u_src(2 * i + 3), ada_at(0, i + 8))
            load(S["u_epi"], 0, lambda q: out_grp(w_out, GM_STEPS - 2 + q // 4, q % 4), None)

            def ffn(l, tag):
                def src(j, q):
                    if q < 4:
                        return up_grp(l, j, q)
                    if q < 8:
                        return out_grp(ffn_w_down[l], j - 1, q - 4)
                    if isinstance(j, int) and j == FF_STEPS - 1:
                        return out_grp(ffn_w_down[l], j, q - 8)
                    return gate_grp(l, j + 1, q - 8)

                def steps(j):
                    return lambda q: src(j + q // 12, q % 12)
                load(S[tag + "_pro"], 0, lambda q: gate_grp(l, 0, q) if q < 4 else
                     up_grp(l, 0, q - 4) if q < 8 else gate_grp(l, 1, q - 8), ada_at(1, 0))
                with sp.Fori(0, 4) as i:
                    load(S[tag], i, steps(2 * i + 1), ada_at(1, i + 1))
                load(S[tag + "_epi"], 0, steps(FF_STEPS - 2), ada_at(1, 5))

            ffn(0, "f0")
            load(S["qkv"], 0, lambda q: tile_of(w_qkv, 512 * (q % 4), 512 * ((q // 4 + 4) % 5)), ada_at(1, 7))
            load(S["attend"], 0, None, ada_at(1, 9))
            load(S["wo"], 0, lambda q: tile_of(w_o, 512 * (q % 4), 512 * (q // 4)), ada_at(1, 11))
            ffn(1, "f1")
            for n in range(4):
                b, cs = n // 2, slice(n % 2 * D // 2, (n % 2 + 1) * D // 2)
                sp.wait_ge(out_ready, n + 1)
                sp.dma_start(out[0, b * P:(b + 1) * P, cs], outs[:, b, cs]).then_inc(stored, 16)
            sp.wait_ge(stored, 64)

        @block.gpsimd
        def _(pool):
            def bias_rows(t):
                for slot in range(2):
                    if not (isinstance(t, int) and t == 0):
                        pool.wait_ge(v_biased, 4 * t + 2 * slot - 2)
                    pool.dma_start(tmp[:, slot, :], gm_b_in[0, bass.ds(E + (2 * t + slot) * 512, 512)]
                                   .partition_broadcast(P)).then_inc(vb_landed[slot], 16)
            bias_rows(0)
            with pool.Fori(1, GM_STEPS // 2) as i:
                bias_rows(i)

            pool.wait_ge(bs_landed, 16)
            for pr in range(ET // 2):
                pool.wait_ge(mix_rs, pr + 1)
                term = terms[:, pr % 4, :, :]
                nc.gpsimd.tensor_tensor(term, term, bs_bc[:, 2 * pr // TPG:2 * pr // TPG + 1, :].to_broadcast([P, 2, P]),
                                        ALU.add).then_inc(mix_t, 1)

            def add_outputs(n0):
                for k in range(8):
                    pool.wait_ge(out_evac, n0 + k + 1)
                    nc.gpsimd.tensor_tensor(xs[:, k % 2, (k // 2) * 512:(k // 2 + 1) * 512],
                                            xs[:, k % 2, (k // 2) * 512:(k // 2 + 1) * 512],
                                            tmp[:, k % 2, :], ALU.add).then_inc(x_added, 1)
            with pool.Fori(0, EV_WO // 8) as i:
                add_outputs(8 * i)
            pool.wait_ge(att_landed, 48)
            for n in range(9):
                pair = (n + 8) % 9
                dst = (qT if pair < 8 else kT)[:, (2 * pair) % 16:(2 * pair) % 16 + 2, :]
                pool.wait_ge(rot_done, n + 1)
                nc.gpsimd.tensor_tensor(dst, dst, trig[:, 0, :].unsqueeze(1).to_broadcast([P, 2, 256]), ALU.mult
                                        ).then_inc(rot_cos, 1)
                pool.wait_ge(rot_cos, n + 1)
                pool.wait_ge(rot_sin, n + 1)
                nc.gpsimd.tensor_tensor(dst, dst, sin_part[n % 2], ALU.add).then_inc(roped, 1)
            pool.wait_ge(gate_evac, 12)
            pool.wait_ge(bo_landed, 16)
            nc.gpsimd.tensor_tensor(bo_bc, bo_bc, gate[:, :], ALU.mult).then_inc(bo_gated, 1)
            pool.wait_ge(bo_gated, 1)
            for b in range(2):
                nc.gpsimd.tensor_tensor(xs[:, b, :], xs[:, b, :], bo_bc, ALU.add).then_inc(bo_added, 1)
            pool.wait_ge(bo_added, 2)
            with pool.Fori(EV_WO // 8, EV_END // 8) as i:
                add_outputs(8 * i)

        @block.scalar
        def _(act):
            act.dma_start(ident[:], consts[:, 0:128]).then_inc(c_landed, 16)
            act.dma_start(crow[0:16, :], c[0].rearrange("(r i) -> r i", i=P)).then_inc(c_landed, 16)
            act.wait_ge(nat_zero, 1)
            small_loads = [
                (nat[16:48, 0, :], mix_norm_g.rearrange("l (r i) -> (l r) i", i=P)),
                (nat[48:80, 0, :], ffn_norm_g.rearrange("l (r i) -> (l r) i", i=P)),
                (nat[80:100, 0, :], sw_b_qkv[0].rearrange("(r i) -> r i", i=P)),
                (nat[0:96, 1, :], ada_b[0].rearrange("(r i) -> r i", i=P)),
                (nat[0:96, 2, :], ada_b[1].rearrange("(r i) -> r i", i=P)),
                (nat[0:48, 3, :], gm_b_in[0, 0:E].rearrange("(r i) -> r i", i=P)),
                (nat[48:96, 3, :], gm_ln_g[0].rearrange("(r i) -> r i", i=P)),
                (nat[0:48, 4, :], gm_ln_b[0].rearrange("(r i) -> r i", i=P)),
                (wsn, gm_w_s[0].rearrange("g i j -> i g j")),
                (negsink[:, :], sw_sinks[0].partition_broadcast(P)),
                (mask32, mask_consts),
            ]
            for dst, src in small_loads:
                act.dma_start(dst, src).then_inc(vec_landed, 16)
            act.dma_start(xs[:, :, :], x[0].rearrange("(b p) d -> p b d", p=P)).then_inc(x_landed, 16)
            act.wait_ge(c_turned, 1)
            nc.scalar.activation(ccol[:, :], ps[:, 7, 0:KD], ACT.Silu).then_inc(cond_ready, 1)
            act.wait_ge(turned, 1)
            nc.scalar.copy(cols[:, 0, :], ps[:, 6, 0:128]).then_inc(table, 1)
            act.wait_ge(turned, 2)
            nc.scalar.copy(cols[:, 1:5, :], ps[:, 5, :].rearrange("p (t i) -> p t i", t=4)).then_inc(table, 1)

            def stage_hi(piece, i, e, q):
                act.wait_ge(raw_landed[e % 4], 16 * (piece.turn(i) + e // 4 + 1))
                for h in range(2):
                    u = piece.unit(i) + 2 * q + h
                    if not (isinstance(u, int) and u < 4):
                        act.wait_ge(unit_done, u - 3)
                    nc.scalar.copy(whi[:, (2 * q + h) % 4], raw[:, e % 4, 2 * h:2 * h + 2, :]).then_inc(hi_ready, 1)

            def stage(piece, i, q):
                stage_hi(piece, i, piece.pos[("W", q)], q)

            def root(n):
                act.wait_ge(ms_ready, n)
                nc.scalar.activation(small[:, 12:14], small[:, 10:12], ACT.Sqrt).then_inc(root_ready, 1)

            def norm_stats(k, n_last, blocks=range(8)):
                if 0 in blocks:
                    nc.scalar.activation(small[:, 52:53], ones[:, 0:1], ACT.Sqrt)
                for m in blocks:
                    ch, b = m // 2, m % 2
                    if n_last is not None:
                        act.wait_ge(x_added, n_last + m + 1)
                    elif m == 0:
                        act.wait_ge(x_landed, 16)
                    nc.scalar.activation(hid[:, 0:2, :], xs[:, b, ch * 512:(ch + 1) * 512].rearrange(
                        "p (a c) -> p a c", a=2), ACT.Square, accum_out=small[:, b * 4 + ch:b * 4 + ch + 1]
                    ).then_inc(sq_ready, 1)
                    act.wait_ge(sq_ready, 8 * k + m + 1)
                if 7 in blocks:
                    root(ROOT[k])

            def norm_hi(k, q):
                m0 = SHIFT[k]
                for kt in range(4 * q, 4 * q + 4):
                    act.wait_ge(h_ready, 16 * k + kt + 1)
                    nc.scalar.activation(hTh[:, kt, :], hid[:, kt % 4, :], ACT.Identity,
                                         bias=mod[:, m0 + kt:m0 + kt + 1]).then_inc(hT_hi, 1)

            def split_hi(step, units):
                if units is not None:
                    act.wait_ge(unit_done, units)
                for m in range(2):
                    act.wait_ge(hid_ready, 2 * step + m + 1)
                    nc.scalar.copy(hidh[:, 2 * m:2 * m + 2, :], hid[:, 2 * m:2 * m + 2, :]).then_inc(hid_hi, 1)

            def gate_rows(b, half, bank):
                for m in range(2):
                    ch = 2 * half + m
                    act.wait_ge(bc_done, 4 * b + ch + 1)
                    nc.scalar.copy(gate[:, ch * 512:(ch + 1) * 512], ps[:, bank + m, :]).then_inc(gate_evac, 1)

            act.wait_ge(ones_ready, 1)
            act.wait_ge(turned, 3)
            nc.scalar.copy(wsT[:, :, :], ps[:, 3:5, :].rearrange("p k (g i) -> p (k g) i", i=P)).then_inc(table, 1)
            act.wait_ge(turned, 4)
            nc.scalar.copy(rs_bc[:, :, :], ps[:, 1:3, :].rearrange("p k (g i) -> p (k g) i", i=P)).then_inc(table, 1)

            norm_stats(0, None)

            def v_gelu_chunk(ch):
                for b in range(2):
                    act.wait_ge(v_biased, 2 * ch + b + 1)
                    vc = vT[:, bass.ds(4 * ch, 4), b, :]
                    nc.scalar.activation(vc, vc, ACT.Gelu).then_inc(v_gelu, 1)

            act.dma_start(gate[:, D - GROUPS * P:],
                          gm_b_s[0].rearrange("g i -> (g i)").partition_broadcast(P)).then_inc(bs_landed, 16)

            def v_body(piece, i, t, first):
                for q in range(16):
                    stage(piece, i, q)
                    start = first and q < 8
                    if start and q < 4:
                        norm_hi(0, q)
                    if q % 8 == 0 and not start:
                        v_gelu_chunk(2 * (t + q // 8) - 1)
                    if q % 8 == 4:
                        v_gelu_chunk(2 * (t + q // 8))
            v_body(S["v_first"], 0, 0, True)
            with act.Fori(0, 2) as i:
                v_body(S["v"], i, 2 * i + 2, False)

            def u_gelu(j, units, split_before):
                act.wait_ge(unit_done, units)
                if split_before:
                    act.wait_ge(hid_lo, 2 * j)
                for m in range(4):
                    ins = nc.scalar.activation(hid[:, m, :], ps[:, WU + m // 2, (m % 2) * 256:(m % 2 + 1) * 256],
                                               ACT.Gelu, bias=bu[:, bass.ds(4 * j + m, 1)])
                    if m % 2:
                        ins.then_inc(gelu_u, 1)
            def v_scale():
                act.wait_ge(ln_ready, 1)
                for k in range(3):
                    part = vT[:, 16 * k:16 * k + 16, 1, :]
                    nc.scalar.activation(part, part, ACT.Identity, bias=small[:, 50:51], scale=small[:, 19:20]
                                         ).then_inc(v_normed_b1, 1)

            def mix_terms():
                act.wait_ge(table, 4)
                act.wait_ge(v_biased, 2 * GM_STEPS)
                for pr in range(ET // 2):
                    if pr >= 4:
                        act.wait_ge(mixed, 2 * (pr - 3))
                    for m in range(2):
                        ti = 2 * pr + m
                        ins = nc.scalar.activation(terms[:, pr % 4, m, :], rs_bc[:, ti // TPG, :], ACT.Identity,
                                                   scale=lnb[:, ti:ti + 1])
                    ins.then_inc(mix_rs, 1)
            for q in range(8):
                stage(S["u_pro"], 0, q)
                if q == 0:
                    v_gelu_chunk(GM_STEPS - 1)
                if q == 1:
                    root(ROOT_LN)
                if q == 3:
                    v_scale()
                if q == 4:
                    u_gelu(0, S["u_pro"].unit() + 8, False)
                if q == 5:
                    mix_terms()
                    split_hi(0, None)
            act.wait_ge(mixed, ET)
            gate_rows(0, 0, WD)
            gate_rows(0, 1, WD + 2)

            def u_body(piece, i, j):
                for q in range(16):
                    stage(piece, i, q)
                    if q % 8 == 0:
                        u_gelu(j + q // 8, piece.unit(i) + 2 * q, True)
                    if q % 8 == 4:
                        split_hi(j + q // 8, piece.unit(i) + 2 * q)
            u_body(S["u_first"], 0, 1)
            with act.Fori(0, 4) as i:
                u_body(S["u"], i, 2 * i + 3)
            L = GM_STEPS - 1
            for q in range(8):
                stage(S["u_epi"], 0, q)
                if q == 0:
                    u_gelu(L, S["u_epi"].unit(), True)
                if q == 4:
                    split_hi(L, S["u_epi"].unit() + 8)

            def ffn(l, tag, k_norm, g_b):
                s0, n0 = STEP_F[l], EV_F[l]

                def silu(j, units, split_before):
                    act.wait_ge(unit_done, units)
                    if split_before:
                        act.wait_ge(hid_lo, 2 * (s0 + j))
                    for m in range(2):
                        nc.scalar.activation(hid[:, 2 * m:2 * m + 2, :].rearrange("p a c -> p (a c)"),
                                             ps[:, WG + m, :], ACT.Silu).then_inc(silu_g, 1)
                pro = S[tag + "_pro"]
                for q in range(12):
                    stage(pro, 0, q)
                    if q == 0:
                        norm_stats(k_norm, n0 - 8, range(6))
                    if q == 1:
                        norm_stats(k_norm, n0 - 8, range(6, 8))
                        norm_hi(k_norm, 0)
                    if 1 <= q < 4:
                        norm_hi(k_norm, q)
                    if q == 4:
                        silu(0, pro.unit() + 8, False)
                    if q == 8:
                        gate_rows(g_b, 0, WD)
                    if q == 9:
                        split_hi(s0, None)
                    if q == 11:
                        gate_rows(g_b, 1, WD + 2)

                def body(piece, i, j):
                    for q in range(24):
                        stage(piece, i, q)
                        if q % 12 == 0:
                            silu(j + q // 12, piece.unit(i) + 2 * q, True)
                        if q % 12 == 8:
                            split_hi(s0 + j + q // 12, piece.unit(i) + 2 * q)
                with act.Fori(0, 4) as i:
                    body(S[tag], i, 2 * i + 1)
                body(S[tag + "_epi"], 0, FF_STEPS - 2)

            ffn(0, "f0", 1, 1)

            att_loads = [(trig, consts[:, 256:768].rearrange("p (t q) -> p t q", t=2)), (rot, consts[:, 128:256]),
                         (vb_bc, sw_b_qkv[0, ATT + KV:ATT + 2 * KV].partition_broadcast(P))]
            for dst, src in att_loads:
                act.dma_start(dst, src).then_inc(att_landed, 16)

            def qk_bias(n, bank):
                pair = (n + 8) % 9
                dst = qT if pair < 8 else kT
                for m in range(2):
                    ins = nc.scalar.activation(dst[:, (2 * pair) % 16 + m, :], ps[:, bank, m * 256:(m + 1) * 256],
                                               ACT.Identity, bias=cols[:, 0, BQKV + 2 * pair + m:BQKV + 2 * pair + m + 1])
                ins.then_inc(q_bias, 1)
            for q in range(20):
                stage(S["qkv"], 0, q)
                if q == 0:
                    norm_stats(2, EV_WO - 8, range(6))
                if q == 1:
                    norm_stats(2, EV_WO - 8, range(6, 8))
                    norm_hi(2, 0)
                if 1 <= q < 4:
                    norm_hi(2, q)
                if q == 7:
                    gate_rows(2, 0, 6)
                if q == 9:
                    gate_rows(2, 1, 6)
                if q >= 4 and q % 4 == 0:
                    act.wait_ge(unit_done, S["qkv"].unit() + 2 * q)
                    if q == 4:
                        qk_bias(0, 0)
                    else:
                        qk_bias(q // 2 - 3, 2 * ((q // 4 - 1) % 2))
                        qk_bias(q // 2 - 2, 2 * ((q // 4 - 1) % 2) + 1)
                if q == 12:
                    for m in range(2):
                        act.wait_ge(dup_done, m + 1)
                        nc.scalar.copy(kdup[:, 2 * m:2 * m + 2, :], ps[:, 6 + m, :].rearrange("p (a q) -> p a q", a=2)
                                       ).then_inc(dup_ready, 1)
            act.wait_ge(unit_done, S["qkv"].unit() + 40)
            qk_bias(7, 0)
            qk_bias(8, 1)

            def exps(Q):
                s, bk = Q % 2, 3 * ((Q + 1) % 2)
                if Q >= 2:
                    act.wait_ge(pt_done, 3 * (Q - 1))
                act.wait_ge(s_max, 2 * (Q + 1))
                for i in range(8):
                    mb, r = i // 4, i % 4
                    src = ps[:, bk, r * 128:(r + 1) * 128] if mb == 0 else \
                        ps[:, bk + 1 + r % 2, (r // 2) * 256:(r // 2 + 1) * 256]
                    dst = prob[:, s, r * 128:(r + 1) * 128] if mb == 0 else \
                        prob[:, s, 512 + r * 256:512 + (r + 1) * 256]
                    nc.scalar.activation(dst, src, ACT.Exp, bias=stat[:, 1, s, i:i + 1], scale=0.125,
                                         accum_out=stat[:, 3, s, i:i + 1]).then_inc(p_exp, 1)
                nc.scalar.activation(stat[:, 4, s, :], stat[:, 2, s, :], ACT.Exp).then_inc(p_exp, 1)

            def att_out(Q):
                bk = 3 * ((Q + 1) % 2)
                if Q >= 1:
                    act.wait_ge(o_done, Q)
                for r in (1, 2):
                    act.wait_ge(pt_done, 3 * Q + r + 1)
                    nc.scalar.copy(probT[:, r], ps[:, bk + r, :].rearrange("p (h q) -> p h q", h=4)).then_inc(pt_a, 1)

            def att_hi(Q):
                act.wait_ge(o_done, Q + 1)
                nc.scalar.copy(hTh[:, 2 * Q:2 * Q + 2, :], ps[:, 6 + Q % 2, :].rearrange("p (t q) -> p t q", t=2)
                               ).then_inc(o_hi, 1)
            NQD = NQ // 4
            exps(0)
            for Q in range(NQD):
                att_out(Q)
                if Q + 1 < NQD:
                    exps(Q + 1)
                att_hi(Q)
                if Q >= NQD - 3 and Q < NQD - 1:
                    stage(S["wo"], 0, Q - (NQD - 3))
            act.wait_ge(s_done, 3 * NQD)
            act.dma_start(bo_bc, sw_b_o[0].partition_broadcast(P)).then_inc(bo_landed, 16)
            for q in range(2, 16):
                stage(S["wo"], 0, q)
            act.dma_start(fg_bc, final_g.partition_broadcast(P)).then_inc(fg_landed, 16)
            ffn(1, "f1", 3, 3)
            norm_stats(4, EV_END - 8)

        @block.vector
        def _(dve):
            chain = [0]

            def link(ins):
                chain[0] += 1
                ins.then_inc(dve_step, 1)
                dve.wait_ge(dve_step, chain[0])

            nc.vector.memset(nat, 0.0).then_inc(nat_zero, 1)
            nc.vector.memset(ones[:], 1.0).then_inc(ones_ready, 1)

            def quarter(piece, i, e):
                return 16 * piece.turn(i) + 4 * e

            def stage_lo(piece, i, e, q):
                for h in range(2):
                    dve.wait_ge(hi_ready, piece.unit(i) + 2 * q + h + 1)
                    s = (2 * q + h) % 4
                    nc.vector.tensor_tensor(wlo[:, s], raw[:, e % 4, 2 * h:2 * h + 2, :], whi[:, s].bitcast(F32),
                                            ALU.subtract).then_inc(raw_used, 2)

            def ada_group(piece, i, e, k):
                dve.wait_ge(raw_landed[e % 4], 16 * (piece.turn(i) + e // 4 + 1))
                slot = (k // 8) % 2
                if k % 8 == 0:
                    red = piece.red(i) + max(k // 8 - 1, 0)
                    if not (isinstance(red, int) and red < 1):
                        dve.wait_ge(ada_reduced, red)
                for kk in range(2):
                    kt = 2 * (k % 8) + kk
                    first = k % 8 == 0 and kk == 0
                    if not first:
                        dve.wait_ge(raw_used, quarter(piece, i, e) + 2 * kk)
                    if first:
                        ins = nc.vector.tensor_scalar(acc[:, slot, :], raw_ada[:, e % 4, kk, :], ccol[:, kt:kt + 1],
                                                      None, ALU.mult)
                    else:
                        ins = nc.vector.scalar_tensor_tensor(out=acc[:, slot, :], in0=raw_ada[:, e % 4, kk, :],
                                                             scalar=ccol[:, kt:kt + 1], in1=acc[:, slot, :],
                                                             op0=ALU.mult, op1=ALU.add)
                    ins.then_inc(raw_used, 2)

            def mod_add(red, layer, unit, n, bank):
                dve.wait_ge(ada_reduced, red + n)
                dst = mod[:, bass.ds(96 * layer + 8 * unit, 8 * n)]
                nc.vector.tensor_tensor(dst, ps[:, bank, 0:8 * n], dst, ALU.add).then_inc(mod_ready, n)

            def run(piece, i, hooks, norm=False, first=0):
                n = len(piece.order)
                for e, (kind, q) in list(enumerate(piece.order))[first:]:
                    if kind == "A":
                        ada_group(piece, i, e, q)
                    else:
                        stage_lo(piece, i, e, q)
                        w = q
                        if norm and w < 4:
                            hooks(w)
                    if (e + 1 == n or piece.order[e + 1][0] == "W") and not (norm and w < 4):
                        hooks(w)

            def inverse_root(n, mean, scale, eps):
                nc.vector.tensor_scalar(small[:, 10:12], mean, scale, eps, ALU.mult, ALU.add).then_inc(ms_ready, 1)
                dve.wait_ge(root_ready, n)
                r0, t, r, a = small[:, 14:16], small[:, 16:18], small[:, 18:20], small[:, 10:12]
                link(nc.vector.reciprocal(r0, small[:, 12:14]))
                link(nc.vector.tensor_tensor(t, r0, r0, ALU.mult))
                link(nc.vector.tensor_tensor(t, t, a, ALU.mult))
                link(nc.vector.tensor_scalar(t, t, -0.5, 1.5, ALU.mult, ALU.add))
                link(nc.vector.tensor_tensor(r, r0, t, ALU.mult))

            def norm_scale(k):
                dve.wait_ge(sq_ready, 8 * (k + 1))
                link(nc.vector.tensor_reduce(small[:, 8:10], small[:, 0:8].rearrange("p (b c) -> p b c", b=2), AX.X, ALU.add))
                inverse_root(ROOT[k], small[:, 8:10], 1.0 / D, EPS_RMS)

            def norm_x(k):
                norm_scale(k)
                for b in range(2):
                    nc.vector.tensor_scalar(rdiag[:, b * P:(b + 1) * P], ident[:, :], small[:, 18 + b:19 + b], None,
                                            ALU.mult).then_inc(rdiag_ready, 1)
                dve.wait_ge(rrow_done, k + 1)
                nc.vector.tensor_copy(rrow, ps[:, 7, 256:512]).then_inc(rrow_taken, 1)
                dve.wait_ge(rrow_taken, k + 1)

            def norm_mod(k, g_col):
                dve.wait_ge(mod_ready, RED_NORM[k])
                m0 = SHIFT[k]
                link(nc.vector.scalar_tensor_tensor(out=amul[:, :], in0=mod[:, m0 + 16:m0 + 32], scalar=1.0,
                                                    in1=cols[:, 0, g_col:g_col + 16], op0=ALU.add, op1=ALU.mult))

            def norm_lo(k, q):
                m0 = SHIFT[k]
                for kt in range(4 * q, 4 * q + 4):
                    dve.wait_ge(nT_ready, 16 * k + 2 * (kt // 2) + 2)
                    if kt >= 4:
                        dve.wait_ge(hT_ready, 16 * k + kt - 3)
                    nc.vector.scalar_tensor_tensor(out=hid[:, kt % 4, :], in0=ps[:, kt // 2, (kt % 2) * 256:(kt % 2 + 1) * 256],
                                                   scalar=amul[:, kt:kt + 1], in1=rrow, op0=ALU.mult, op1=ALU.mult
                                                   ).then_inc(h_ready, 1)
                for kt in range(4 * q, 4 * q + 4):
                    dve.wait_ge(hT_hi, 16 * k + kt + 1)
                    nc.vector.scalar_tensor_tensor(out=hTl[:, kt, :], in0=hid[:, kt % 4, :],
                                                   scalar=mod[:, m0 + kt:m0 + kt + 1], in1=hTh[:, kt, :].bitcast(F32),
                                                   op0=ALU.add, op1=ALU.subtract).then_inc(hT_ready, 1)

            def split_lo(step):
                for m in range(2):
                    dve.wait_ge(hid_hi, 2 * step + m + 1)
                    nc.vector.tensor_tensor(hidl[:, 2 * m:2 * m + 2, :], hid[:, 2 * m:2 * m + 2, :],
                                            hidh[:, 2 * m:2 * m + 2, :].bitcast(F32), ALU.subtract).then_inc(hid_lo, 1)

            def evac(n0, ch, units):
                dve.wait_ge(unit_done, units)
                for b in range(2):
                    k = 2 * ch + b
                    if not (isinstance(n0, int) and n0 + k < 2):
                        dve.wait_ge(x_added, n0 + k - 1)
                    nc.vector.tensor_tensor(tmp[:, b, :], ps[:, WD + k % 4, :], gate[:, ch * 512:(ch + 1) * 512],
                                            ALU.mult).then_inc(out_evac, 1)

            def diagonals(b, half, src):
                if half == 0:
                    dve.wait_ge(mod_ready, RED_GATE[b])
                if 4 * b + 2 * half:
                    dve.wait_ge(bc_done, 4 * b + 2 * half)
                for ch in (2 * half, 2 * half + 1):
                    for m in range(4):
                        ins = nc.vector.tensor_scalar(tmp[:, ch % 2, m * P:(m + 1) * P], ident[:, :],
                                                      src[:, 4 * ch + m:4 * ch + m + 1], None, ALU.mult)
                    ins.then_inc(diag_ready, 1)

            dve.wait_ge(cond_ready, 1)

            def small_tables():
                dve.wait_ge(table, 2)
                link(nc.vector.tensor_copy(mod[:, :].rearrange("p (l k) -> p l k", l=2), adab))
                dve.wait_ge(table, 3)
                nc.vector.memset(wsT[64:128, :, 0:64], 0.0).then_inc(ws_ready, 1)
                link(nc.vector.tensor_scalar(negsink[:, :], negsink[:, :], -1.0, None, ALU.mult))
                link(nc.vector.tensor_copy(maskc[:, :], mask32))
            for e in range(32):
                ada_group(S["start"], 0, e, e)
                if e == 7:
                    small_tables()
                if e == 15:
                    norm_x(0)

            def v_bias(t, slot, units):
                ch = 2 * t + slot
                dve.wait_ge(vb_landed[slot], 16 * t + 16)
                dve.wait_ge(unit_done, units)
                for b in range(2):
                    nc.vector.tensor_tensor(vT[:, bass.ds(4 * ch, 4), b, :],
                                            ps[:, 4 * slot + b, :].rearrange("p (t i) -> p t i", t=4),
                                            tmp[:, slot, :].rearrange("p (t i) -> p t i", t=4), ALU.add
                                            ).then_inc(v_biased, 1)

            def v_stat(ch):
                for b in range(2):
                    dve.wait_ge(v_gelu, 2 * ch + b + 1)
                    for_chunk = vT[:, bass.ds(4 * ch, 4), b, :]
                    nc.vector.bn_stats(vst[:, b, bass.ds(ch, 1), :].rearrange("p a s -> p (a s)"), for_chunk).then_inc(v_stats, 1)

            def v_hooks(piece, i, t, unit, first):
                units = piece.unit(i)

                def hooks(q):
                    pair = t + q // 8
                    start = first and q < 8
                    if start and q == 0:
                        mod_add(0, 0, 0, 4, ADA_BANK["start"])
                        norm_mod(0, MIXG)
                    if start and q < 4:
                        norm_lo(0, q)
                    if q % 8 == 0 and not start:
                        v_bias(pair - 1, 1, units + 2 * q)
                    if q % 8 == 1 and not start:
                        v_stat(2 * pair - 1)
                    if q % 8 == 4:
                        v_bias(pair, 0, units + 2 * q)
                    if q % 8 == 5:
                        v_stat(2 * pair)
                    if q == 15:
                        mod_add(piece.red(i), 0, unit, 1, ADA_BANK["v"])
                return hooks
            run(S["v_first"], 0, v_hooks(S["v_first"], 0, 0, 4, True), norm=True)
            with dve.Fori(0, 2) as i:
                run(S["v"], i, v_hooks(S["v"], i, 2 * i + 2, i + 5, False))

            def u_mul(j):
                for m in range(2):
                    dve.wait_ge(gelu_u, 2 * j + m + 1)
                    nc.vector.tensor_tensor(hid[:, 2 * m:2 * m + 2, :], hid[:, 2 * m:2 * m + 2, :],
                                            vT[:, bass.ds(4 * j + 2 * m, 2), :, :].rearrange("p t b i -> p t (b i)"),
                                            ALU.mult).then_inc(hid_ready, 1)

            def v_layer_norm():
                dve.wait_ge(v_stats, 2 * GM_STEPS)
                for b in range(2):
                    link(nc.vector.bn_aggr(small[:, 20 + 2 * b:22 + 2 * b], vst[:, b, :, :].rearrange("p a s -> p (a s)")))
                inverse_root(ROOT_LN, small[:, 21:24:2], 1.0, EPS_LN)

                nc.vector.tensor_scalar(small[:, 50:51], small[:, 22:23], small[:, 19:20], -1.0, ALU.mult, ALU.mult
                                        ).then_inc(ln_ready, 1)

            def v_scale():
                for k in range(3):
                    part = vT[:, 16 * k:16 * k + 16, 0, :]
                    nc.vector.tensor_scalar(part, part, small[:, 20:21], small[:, 18:19],
                                            ALU.subtract, ALU.mult).then_inc(v_normed, 1)

            def mix_out():
                for pr in range(ET // 2):
                    dve.wait_ge(mix_t, pr + 1)
                    dve.wait_ge(mix_done, pr + 1)
                    for m in range(2):
                        ti = 2 * pr + m
                        nc.vector.scalar_tensor_tensor(
                            out=vT[:, ti, :, :], in0=ps[:, WD + pr % 4, m * 256:(m + 1) * 256].rearrange("p (b i) -> p b i", b=2),
                            scalar=lng[:, ti:ti + 1],
                            in1=terms[:, pr % 4, m, :].unsqueeze(1).to_broadcast([P, 2, P]),
                            op0=ALU.mult, op1=ALU.add).then_inc(mixed, 1)

            def u_pro_hooks(q):
                if q == 0:
                    v_bias(GM_STEPS // 2 - 1, 1, S["u_pro"].unit())
                if q == 1:
                    v_stat(GM_STEPS - 1)
                    v_layer_norm()
                if q == 2:
                    v_scale()
                if q == 5:
                    mix_out()
                    u_mul(0)
                    split_lo(0)
                if q >= 6:
                    diagonals(0, q - 6, mod[:, 32:48])
            run(S["u_pro"], 0, u_pro_hooks)

            def u_hooks(piece, i, j, unit):
                units = piece.unit(i)

                def hooks(q):
                    step, r = j + q // 8, q % 8
                    if r == 1:
                        dve.wait_ge(mixed, ET)
                        u_mul(step)
                    if 1 <= r <= 4:
                        evac(8 * (step - 1), r - 1, units + 2 * q)
                    if r == 4:
                        split_lo(step)
                    if q == 15:
                        mod_add(piece.red(i), 0, unit, 1, ADA_BANK["u"])
                return hooks
            run(S["u_first"], 0, u_hooks(S["u_first"], 0, 1, 7))
            with dve.Fori(0, 4) as i:
                run(S["u"], i, u_hooks(S["u"], i, 2 * i + 3, i + 8))
            L = GM_STEPS - 1

            def u_epi_hooks(q):
                if q == 1:
                    u_mul(L)
                if 1 <= q <= 4:
                    evac(8 * (L - 1), q - 1, S["u_epi"].unit() + 2 * q)
                if q == 4:
                    split_lo(L)
                if q >= 5:
                    evac(8 * L, q - 5, S["u_epi"].unit() + 2 * q)
            run(S["u_epi"], 0, u_epi_hooks)

            def ffn(l, tag, k_norm, g_b):
                s0, n0 = STEP_F[l], EV_F[l]

                def up_mul(j, units):
                    dve.wait_ge(unit_done, units)
                    for m in range(2):
                        dve.wait_ge(silu_g, 2 * (l * FF_STEPS + j) + m + 1)
                        half = hid[:, 2 * m:2 * m + 2, :].rearrange("p a c -> p (a c)")
                        nc.vector.tensor_tensor(half, half, ps[:, WU + m, :], ALU.mult).then_inc(hid_ready, 1)

                def pro_hooks(q):
                    if q == 0:
                        evac(n0 - 8, 3, S[tag + "_pro"].unit())
                    if q == 1:
                        norm_x(k_norm)
                        norm_mod(k_norm, FFNG + 16 * l)
                        norm_lo(k_norm, 0)
                    if 1 <= q < 4:
                        norm_lo(k_norm, q)
                    if q == 5 or q == 8:
                        diagonals(g_b, q // 8, mod[:, 96 * l + 80:96 * l + 96])
                    if q == 9:
                        up_mul(0, S[tag + "_pro"].unit() + 16)
                        split_lo(s0)
                    if q == 11 and S[tag + "_pro"].n_ada:
                        mod_add(S[tag + "_pro"].red(), 1, 0, S[tag + "_pro"].n_red, ADA_BANK["ffn"])
                run(S[tag + "_pro"], 0, pro_hooks, norm=True)

                def hooks_of(piece, i, j, unit):
                    units = piece.unit(i)

                    def hooks(q):
                        step, r = j + q // 12, q % 12
                        if r == 5:
                            up_mul(step, units + 2 * q - 2)
                        if 5 <= r <= 8:
                            evac(n0 + 8 * (step - 1), r - 5, units + 2 * q)
                        if r == 8:
                            split_lo(s0 + step)
                        if q == 23 and piece.n_ada:
                            mod_add(piece.red(i), 1, unit, piece.n_red, ADA_BANK["ffn"])
                    return hooks
                with dve.Fori(0, 4) as i:
                    run(S[tag], i, hooks_of(S[tag], i, 2 * i + 1, i + 1))
                J, epi = FF_STEPS - 1, S[tag + "_epi"]

                def epi_hooks(q):
                    hooks_of(epi, 0, J - 1, 5)(q)
                    if q >= 21:
                        evac(n0 + 8 * J, q - 21, epi.unit() + 2 * q)
                run(epi, 0, epi_hooks)

            ffn(0, "f0", 1, 1)

            def rope(n):
                sinb = trig[:, 1, :].unsqueeze(1).to_broadcast([P, 2, 256])
                dve.wait_ge(rot_done, n + 1)
                if n >= 2:
                    dve.wait_ge(roped, n - 1)
                nc.vector.tensor_tensor(sin_part[n % 2], ps[:, rot_bank(n), :].rearrange("p (t q) -> p t q", t=2), sinb,
                                        ALU.mult).then_inc(rot_sin, 1)

            def qkv_hooks(q):
                if q == 0:
                    evac(EV_WO - 8, 3, S["qkv"].unit())
                if q == 1:
                    norm_x(2)
                    norm_mod(2, MIXG + 16)
                    norm_lo(2, 0)
                if 1 <= q < 4:
                    norm_lo(2, q)
                if q == 4:
                    dve.wait_ge(att_landed, 48)
                if q == 4 or q == 7:
                    diagonals(2, q // 7, mod[:, 96 + 32:96 + 48])
                if q == 5:
                    dve.wait_ge(unit_done, S["qkv"].unit() + 8)
                    nc.vector.tensor_tensor(vtok[:, :, :], ps[:, 1, :].rearrange("p (b d) -> p b d", b=2),
                                            vb_bc.unsqueeze(1).to_broadcast([P, 2, 256]), ALU.add).then_inc(vtok_ready, 1)
                    rope(0)
                if q >= 9 and q % 4 == 1:
                    rope(q // 2 - 3)
                    rope(q // 2 - 2)
                if q == 19:
                    mod_add(S["qkv"].red(), 1, 7, 2, 7)
            run(S["qkv"], 0, qkv_hooks, norm=True)

            def attend_groups(lo, hi):
                for e in range(lo, hi):
                    ada_group(S["attend"], 0, e, e)
            attend_groups(0, 4)

            def quad_max(Q):
                s, bk = Q % 2, 3 * ((Q + 1) % 2)
                for k, r in enumerate((1, 2, 0)):
                    dve.wait_ge(s_done, 3 * Q + k + 1)
                    dst, src = (stat[:, 0, s, 0:4], ps[:, bk, :].rearrange("p (h k) -> p h k", h=4)) if r == 0 else \
                        (stat[:, 0, s, 3 + r:8:2], ps[:, bk + r, :].rearrange("p (h k) -> p h k", h=2))
                    ins = nc.vector.tensor_reduce(dst, src, AX.X, ALU.max)
                    link(ins)
                ns = negsink[:, 4 * Q:4 * Q + 4].unsqueeze(1).to_broadcast([P, 2, 4])
                two = lambda k: stat[:, k, s, :].rearrange("p (m h) -> p m h", m=2)
                nc.vector.scalar_tensor_tensor(out=two(1), in0=two(0), scalar=-0.125, in1=ns,
                                               op0=ALU.mult, op1=ALU.min).then_inc(s_max, 1)
                dve.wait_ge(s_max, 2 * Q + 1)
                nc.vector.tensor_tensor(two(2), two(1), ns, ALU.subtract).then_inc(s_max, 1)

            def quad_norm(Q):
                s = Q % 2
                dve.wait_ge(p_exp, 9 * (Q + 1))
                link(nc.vector.tensor_tensor(stat[:, 5, s, :], stat[:, 3, s, :], stat[:, 4, s, :], ALU.add))
                link(nc.vector.reciprocal(stat[:, 6, s, :], stat[:, 5, s, :]))
                for i in range(8):
                    mb, r = i // 4, i % 4
                    pp = prob[:, s, r * 128:(r + 1) * 128] if mb == 0 else prob[:, s, 512 + r * 256:512 + (r + 1) * 256]
                    nc.vector.tensor_scalar(pp, pp, stat[:, 6, s, i:i + 1], None, ALU.mult).then_inc(p_norm, 1)

            def quad_out(Q):
                bk = 3 * ((Q + 1) % 2)
                if Q >= 1:
                    dve.wait_ge(o_done, Q)
                dve.wait_ge(pt_done, 3 * Q + 1)
                nc.vector.tensor_copy(probT[:, 0], ps[:, bk, :].rearrange("p (h q) -> p h q", h=4)).then_inc(pt_v, 1)

            def quad_lo(Q):
                dve.wait_ge(o_hi, Q + 1)
                nc.vector.tensor_tensor(hTl[:, 2 * Q:2 * Q + 2, :], ps[:, 6 + Q % 2, :].rearrange("p (t q) -> p t q", t=2),
                                        hTh[:, 2 * Q:2 * Q + 2, :].bitcast(F32), ALU.subtract).then_inc(o_lo, 1)
            NQD = NQ // 4
            quad_max(0)
            rope(7)
            rope(8)
            for Q in range(NQD):
                quad_norm(Q)
                if Q + 1 < NQD:
                    quad_max(Q + 1)
                else:
                    stage_lo(S["wo"], 0, 1, 1)
                quad_out(Q)
                if Q < NQD - 2:
                    attend_groups(4 + 2 * Q, 6 + 2 * Q)
                elif Q == NQD - 2:
                    stage_lo(S["wo"], 0, 0, 0)
                quad_lo(Q)
            def wo_hooks(q):
                if q >= 4 and q % 4 == 0:
                    evac(EV_WO, q // 4 - 1, S["wo"].unit() + 2 * q)
                if q == 3:
                    mod_add(S["attend"].red(), 1, 9, 2, 0)
                if q == 15:
                    mod_add(S["wo"].red(), 1, 11, 1, 0)
            run(S["wo"], 0, wo_hooks, first=2)
            ffn(1, "f1", 3, 3)
            evac(EV_END - 8, 3, S["f1"].unit(4) + 48)

            dve.wait_ge(fg_landed, 16)
            norm_scale(4)
            for n in range(4):
                b, cs = n // 2, slice(n % 2 * D // 2, (n % 2 + 1) * D // 2)
                nc.vector.scalar_tensor_tensor(out=outs[:, b, cs], in0=xs[:, b, cs], scalar=small[:, 18 + b:19 + b],
                                               in1=fg_bc[:, cs], op0=ALU.mult, op1=ALU.mult).then_inc(out_ready, 1)

        @block.tensor
        def _(pe):
            mm = nc.tensor.matmul

            pe.wait_ge(c_landed, 32)
            nc.tensor.transpose(ps[:, 7, 0:KD], crow, ident[0:16, 0:16]).then_inc(c_turned, 1)
            pe.wait_ge(vec_landed, 16 * 11)
            nc.tensor.transpose(ps[:, 6, 0:P], nat[:, 0, :], ident[:, :]).then_inc(turned, 1)
            for t in range(1, 5):
                ins = nc.tensor.transpose(ps[:, 5, (t - 1) * P:t * P], nat[:, t, :], ident[:, :])
            ins.then_inc(turned, 1)
            for g in range(GROUPS):
                ins = nc.tensor.transpose(ps[:, 3 + g // 4, (g % 4) * P:(g % 4 + 1) * P], wsn[:, g, :], ident[:, :])
            ins.then_inc(turned, 1)
            pe.wait_ge(ws_ready, 1)
            pe.wait_ge(ones_ready, 1)
            for m in range(2):
                ins = mm(ps[:, 1 + m, :], ones[:, :], wsT[:, 4 * m:4 * m + 4, :].rearrange("p g i -> p (g i)"), start=True, stop=True)
            ins.then_inc(turned, 1)

            def ada_reduce(piece, i, n, bank, first=0):
                e = piece.pos[("A", 8 * (first + n) - 1)]
                pe.wait_ge(raw_used, 16 * piece.turn(i) + 4 * e + 4)
                red = piece.red(i)
                if not (isinstance(red, int) and red < 1):
                    pe.wait_ge(mod_ready, red)
                for k in range(8 * first, 8 * (first + n)):
                    ins = mm(ps[:, bank, k:k + 1], acc[:, (k // 8) % 2, (k % 8) * P:(k % 8 + 1) * P], ones[:, 0:1],
                             start=True, stop=True)
                    if k % 8 == 7:
                        ins.then_inc(ada_reduced, 1)

            def staged(piece, i, q, h):
                pe.wait_ge(raw_used, 16 * piece.turn(i) + 4 * piece.pos[("W", q)] + 2 * h + 2)
                return (2 * q + h) % 4

            def finish_unit(ins):
                ins.then_inc(unit_done, 1)

            def feature_major(piece, i, q0, bank, h_base=None, tiles=4, ahead=None):
                if h_base is not None:
                    pe.wait_ge(h_ready, h_base + 4)
                for g in range(4):
                    if ahead is not None:
                        ahead(q0 + g)
                    for h in range(2):
                        s = staged(piece, i, q0 + g, h)
                        for kk in range(2):
                            kt = 4 * g + 2 * h + kk
                            if h_base is not None:
                                pe.wait_ge(hT_ready, h_base + kt + 1)
                            for m in range(tiles):
                                o = ps[:, bank + m // 2, (m % 2) * 256:(m % 2 + 1) * 256]
                                a = slice(m * P, (m + 1) * P)
                                mm(o, whi[:, s, kk, a], hTh[:, kt, :], start=(kt == 0 and m % 2 == 0), stop=False)
                                mm(o, whi[:, s, kk, a], hTl[:, kt, :], start=False, stop=False)
                                ins = mm(o, wlo[:, s, kk, a], hTh[:, kt, :], start=False,
                                         stop=(kt == KD - 1 and m % 2 == 1))
                            if tiles == 2:
                                for b in range(2):
                                    o, a = ps[:, bank + 1, b * 256:(b + 1) * 256], slice(b * P, (b + 1) * P)
                                    mm(o, hTh[:, kt, a], whi[:, s, kk, 256:512], start=(kt == 0 and b == 0), stop=False)
                                    mm(o, hTh[:, kt, a], wlo[:, s, kk, 256:512], start=False, stop=False)
                                    ins = mm(o, hTl[:, kt, a], whi[:, s, kk, 256:512], start=False,
                                             stop=(kt == KD - 1 and b == 1))
                        finish_unit(ins)

            def token_major(piece, i, q0, groups, lh, ll, banks, free=None, h_base=None, ahead=None):
                if h_base is not None:
                    pe.wait_ge(h_ready, h_base + 4)
                for g in range(groups):
                    if ahead is not None:
                        ahead(q0 + g)
                    for h in range(2):
                        s = staged(piece, i, q0 + g, h)
                        for b in range(2):
                            if g == 0 and h == 0 and free is not None:
                                free(b)
                            for kk in range(2):
                                kt = 4 * g + 2 * h + kk
                                if h_base is not None and b == 0:
                                    pe.wait_ge(hT_ready, h_base + kt + 1)
                                o, a = ps[:, banks + b, :], slice(b * P, (b + 1) * P)
                                mm(o, lh[:, kt, a], whi[:, s, kk, :], start=(kt == 0), stop=False)
                                mm(o, lh[:, kt, a], wlo[:, s, kk, :], start=False, stop=False)
                                ins = mm(o, ll[:, kt, a], whi[:, s, kk, :], start=False, stop=(kt == 4 * groups - 1))
                        finish_unit(ins)

            def turn_x(k, tiles, n_last=None):
                for kt in tiles:
                    if n_last is not None and kt % 4 == 0:
                        pe.wait_ge(x_added, n_last + 2 * (kt // 4) + 2)
                    for b in range(2):
                        ins = nc.tensor.transpose(ps[:, kt // 2, (kt % 2) * 256 + b * P:(kt % 2) * 256 + (b + 1) * P],
                                                  xs[:, b, kt * P:(kt + 1) * P], ident[:, :])
                    ins.then_inc(nT_ready, 1)

            def scale_row(k):
                pe.wait_ge(rdiag_ready, 2 * k + 2)
                mm(ps[:, 7, 256:512], ones[:, :], rdiag, start=True, stop=True).then_inc(rrow_done, 1)
                pe.wait_ge(rrow_taken, k + 1)

            def turn_all(k, n_last):
                pe.wait_ge(mod_ready, RED_NORM[k])
                turn_x(k, range(KD - 2), n_last)
                scale_row(k)
                turn_x(k, range(KD - 2, KD), n_last)

            def output_chunk(piece, i, q, n0, ch, groups=1, lh=hidh, ll=hidl, ahead=None):
                def free(b):
                    n = n0 + 2 * ch + b
                    if not (isinstance(n, int) and n < 4):
                        pe.wait_ge(out_evac, n - 3)
                token_major(piece, i, q, groups, lh, ll, WD + 2 * (ch % 2), free, ahead=ahead)

            def rows_of(b, half, bank):
                for m in range(2):
                    pe.wait_ge(diag_ready, 4 * b + 2 * half + m + 1)
                    mm(ps[:, bank + m, :], ones[:, :], tmp[:, m, :], start=True, stop=True).then_inc(bc_done, 1)

            ada_reduce(S["start"], 0, 1, ADA_BANK["start"])
            scale_row(0)
            for n in (1, 2):
                ada_reduce(S["start"], 0, 1, ADA_BANK["start"], first=n)
            pe.wait_ge(table, 4)
            turn_x(0, range(KD - 2))
            ada_reduce(S["start"], 0, 1, ADA_BANK["start"], first=3)
            pe.wait_ge(mod_ready, 4)
            turn_x(0, range(KD - 2, KD))

            def v_body(piece, i, t):
                def ahead(q):
                    if q == 15:
                        ada_reduce(piece, i, 1, ADA_BANK["v"])
                for s in range(2):
                    first = isinstance(t, int) and s == 0
                    if not first:
                        pe.wait_ge(v_biased, 4 * (t + s) - 2)
                    token_major(piece, i, 8 * s, 4, hTh, hTl, 0, h_base=0 if first else None)
                    if not first:
                        pe.wait_ge(v_biased, 4 * (t + s))
                    token_major(piece, i, 8 * s + 4, 4, hTh, hTl, 4, ahead=ahead)
            v_body(S["v_first"], 0, 0)
            with pe.Fori(0, 2) as i:
                v_body(S["v"], i, 2 * i + 2)

            feature_major(S["u_pro"], 0, 0, WU)
            pe.wait_ge(v_biased, 2 * GM_STEPS)
            pe.wait_ge(v_normed, 3)
            pe.wait_ge(v_normed_b1, 3)
            for pr in range(ET // 2):
                if pr >= 4:
                    pe.wait_ge(mixed, 2 * (pr - 3))
                for m in range(2):
                    ti = 2 * pr + m
                    for b in range(2):
                        ins = mm(ps[:, WD + pr % 4, m * 256 + b * P:m * 256 + (b + 1) * P], vT[:, ti, b, :],
                                 wsT[:, ti // TPG, :], start=True, stop=True)
                ins.then_inc(mix_done, 1)
            pe.wait_ge(gelu_u, 2)

            def mixer_gate(q):
                if q == 7:
                    pe.wait_ge(mixed, ET)
                    rows_of(0, 0, WD)
            feature_major(S["u_pro"], 0, 4, WU, ahead=mixer_gate)
            rows_of(0, 1, WD + 2)
            pe.wait_ge(gate_evac, 4)

            def u_body(piece, i, j):
                def ahead(q):
                    if q == 15:
                        ada_reduce(piece, i, 1, ADA_BANK["u"])
                for s in range(2):
                    pe.wait_ge(hid_lo, 2 * (j + s))
                    for ch in range(4):
                        output_chunk(piece, i, 8 * s + ch, 8 * (j + s - 1), ch)
                    pe.wait_ge(gelu_u, 2 * (j + s) + 2)
                    feature_major(piece, i, 8 * s + 4, WU, ahead=ahead)
            u_body(S["u_first"], 0, 1)
            with pe.Fori(0, 4) as i:
                u_body(S["u"], i, 2 * i + 3)
            for k in range(2):
                pe.wait_ge(hid_lo, 2 * (GM_STEPS - 1 + k))
                for ch in range(4):
                    output_chunk(S["u_epi"], 0, 4 * k + ch, 8 * (GM_STEPS - 2 + k), ch)

            def ffn(l, tag, k_norm, g_b):
                s0, n0, g0 = STEP_F[l], EV_F[l], 2 * l * FF_STEPS
                turn_all(k_norm, n0 - 8)

                def reduce_at(piece, i, step):
                    def ahead(q):
                        if q == piece.n_w - 1 and piece.n_ada:
                            pe.wait_ge(hid_ready, 2 * step + 2)
                            ada_reduce(piece, i, piece.n_red, ADA_BANK["ffn"])
                    return ahead
                pro, epi = S[tag + "_pro"], S[tag + "_epi"]
                feature_major(pro, 0, 0, WG, h_base=16 * k_norm)
                feature_major(pro, 0, 4, WU, ahead=lambda q: rows_of(g_b, 0, WD) if q == 7 else None)
                pe.wait_ge(silu_g, g0 + 2)
                reduce = reduce_at(pro, 0, s0)

                def ahead(q):
                    if q == 10:
                        rows_of(g_b, 1, WD + 2)
                    reduce(q)
                feature_major(pro, 0, 8, WG, ahead=ahead)
                pe.wait_ge(gate_evac, 4 * g_b + 4)

                def up_down(piece, i, q, j):
                    if q == 0:
                        pe.wait_ge(mod_ready, piece.red(i))
                    pe.wait_ge(hid_ready, 2 * (s0 + j))
                    feature_major(piece, i, q, WU)
                    pe.wait_ge(hid_lo, 2 * (s0 + j))
                    for ch in range(4):
                        output_chunk(piece, i, q + 4 + ch, n0 + 8 * (j - 1), ch)

                def gate_half(piece, i, q, j):
                    pe.wait_ge(silu_g, g0 + 2 * j + 2)
                    feature_major(piece, i, q + 8, WG, ahead=reduce_at(piece, i, s0 + j))
                with pe.Fori(0, 4) as i:
                    for s in range(2):
                        up_down(S[tag], i, 12 * s, 2 * i + 1 + s)
                        gate_half(S[tag], i, 12 * s, 2 * i + 1 + s)
                up_down(epi, 0, 0, FF_STEPS - 2)
                gate_half(epi, 0, 0, FF_STEPS - 2)
                up_down(epi, 0, 12, FF_STEPS - 1)
                pe.wait_ge(hid_lo, 2 * (s0 + FF_STEPS))
                last = reduce_at(epi, 0, s0 + FF_STEPS - 1)
                for ch in range(4):
                    last(20 + ch)
                    output_chunk(epi, 0, 20 + ch, n0 + 8 * (FF_STEPS - 1), ch)
            ffn(0, "f0", 1, 1)

            turn_all(2, EV_WO - 8)

            def rotated(n):
                pe.wait_ge(q_bias, n + 1)
                if n >= 4:
                    pe.wait_ge(rot_sin, n - 1 if n == 8 else n - 3)
                pair = (n + 8) % 9
                src = (qT if pair < 8 else kT)[:, (2 * pair) % 16:(2 * pair) % 16 + 2, :]
                mm(ps[:, rot_bank(n), :], rot, src.rearrange("p t q -> p (t q)"), start=True, stop=True).then_inc(rot_done, 1)

            def duplicate_k():
                pe.wait_ge(roped, 1)
                pe.wait_ge(rot_sin, 3)
                for g in range(4):
                    for half in range(2):
                        ins = mm(ps[64 * half:64 * half + 64, 6 + g // 2, (g % 2) * 256:(g % 2 + 1) * 256],
                                 ident[:, (g % 2) * 64:(g % 2) * 64 + 64], kT[:, g // 2, :], start=True, stop=True)
                    if g % 2:
                        ins.then_inc(dup_done, 1)

            def between(q):
                if q == 5:
                    pe.wait_ge(att_landed, 48)
                    rotated(0)
                if q in (6, 8):
                    if q == 8:
                        pe.wait_ge(gate_evac, 10)
                    rows_of(2, q // 8, 6)
                if q == 9:
                    pe.wait_ge(gate_evac, 12)
                if q == 11:
                    duplicate_k()
                if q == 13:
                    pe.wait_ge(dup_ready, 2)
                if q >= 9 and q % 4 == 1:
                    rotated(q // 2 - 3)
                    rotated(q // 2 - 2)
                if q == 19:
                    pe.wait_ge(rot_sin, 4)
                    ada_reduce(S["qkv"], 0, 2, 7)
            for c in range(5):
                if c >= 2:
                    pe.wait_ge(q_bias, 2 * c - 3)
                if c == 2:
                    pe.wait_ge(vtok_ready, 1)
                feature_major(S["qkv"], 0, 4 * c, 2 * (c % 2), h_base=32 if c == 0 else None,
                              tiles=2 if c == 0 else 4, ahead=between)

            def scores(Q):
                bk, g = 3 * ((Q + 1) % 2), Q // 2
                if Q >= 2:
                    pe.wait_ge(pt_v, Q - 1)
                    pe.wait_ge(pt_a, 2 * (Q - 1))
                for r in range(3):
                    mrow, n = (maskc[:, 128:256], 4) if r == 0 else (maskc[:, 256:512], 2)
                    mm(ps[:, bk + r, :].rearrange("p (h k) -> p h k", h=n), maskc[:, 0:128],
                       mrow.unsqueeze(1).to_broadcast([2, n, 512 // n]), start=True, stop=False)

                def head(hh, block):
                    half = slice(64 * (hh % 2), 64 * (hh % 2) + 64)
                    o = ps[:, bk, hh * 128:hh * 128 + 128] if block == 0 else \
                        ps[:, bk + 1 + hh % 2, (hh // 2) * 256:(hh // 2) * 256 + 256]
                    return mm(o, qT[half, 2 * Q + hh // 2, block * P:(block + 1) * P], kdup[half, g, 0:P * (block + 1)],
                              start=False, stop=(hh == 3 if block == 0 else hh >= 2))
                head(0, 0)
                head(2, 0).then_inc(s_even, 1)
                for hh in (0, 2, 1, 3):
                    ins = head(hh, 1)
                    if hh >= 2:
                        ins.then_inc(s_done, 1)
                pe.wait_ge(s_even, Q + 1)
                head(1, 0)
                head(3, 0).then_inc(s_done, 1)

            def attend(Q):
                bk, s, g = 3 * ((Q + 1) % 2), Q % 2, Q // 2
                pe.wait_ge(p_norm, 8 * (Q + 1))
                for r in range(3):
                    for b in range(4):
                        col = b * P if r == 0 else 512 + (2 * (r - 1) + b // 2) * 256 + (b % 2) * P
                        ins = nc.tensor.transpose(ps[:, bk + r, b * P:(b + 1) * P], prob[:, s, col:col + P], ident[:, :])
                    ins.then_inc(pt_done, 1)
                pe.wait_ge(pt_v, Q + 1)
                pe.wait_ge(pt_a, 2 * (Q + 1))
                if Q >= 2:
                    pe.wait_ge(o_lo, Q - 1)
                for hh in range(4):
                    vcol = slice(g * 64, g * 64 + 64)
                    for mb in range(2):
                        o = ps[64 * (hh % 2):64 * (hh % 2) + 64, 6 + s, (hh // 2) * 256 + mb * P:(hh // 2) * 256 + (mb + 1) * P]
                        for kb in range(mb + 1):
                            pt = probT[:, 0, hh, :] if mb == 0 else probT[:, 1 + hh // 2, 2 * (hh % 2) + kb, :]
                            ins = mm(o, vtok[:, kb, vcol], pt, start=(hh < 2 and mb == 0),
                                     stop=(hh >= 2 and mb == 1 and kb == 1))
                ins.then_inc(o_done, 1)
            NQD = NQ // 4
            pe.wait_ge(rot_sin, 7)
            pe.wait_ge(roped, 7)
            scores(0)
            pe.wait_ge(mod_ready, S["qkv"].red() + 2)
            rotated(7)
            rotated(8)
            pe.wait_ge(roped, 9)
            for Q in range(NQD - 1):
                scores(Q + 1)
                attend(Q)

            def wo_ahead(q):
                if q == 1:
                    attend(NQD - 1)
                if q < 4:
                    pe.wait_ge(o_lo, 2 * q + 2)
                if q == 2:
                    ada_reduce(S["attend"], 0, 2, 0)
                if q == 15:
                    ada_reduce(S["wo"], 0, 1, 0)
            for ch in range(4):
                output_chunk(S["wo"], 0, 4 * ch, EV_WO, ch, groups=4, lh=hTh, ll=hTl, ahead=wo_ahead)
            ffn(1, "f1", 3, 3)


_INS = ["x", "c", "ada_w", "ada_b", "mix_norm_g", "ffn_norm_g", "gm_w_in", "gm_b_in", "gm_ln_g", "gm_ln_b", "gm_w_s",
        "gm_b_s", "gm_w_out", "sw_w_qkv", "sw_b_qkv", "sw_sinks", "sw_w_o", "sw_b_o", "ffn_w_gu", "ffn_w_down", "final_g"]


def _constants():
    import numpy as np

    f = np.float32
    ident = np.eye(128, dtype=f)
    rot = np.zeros((128, 128), f)
    for m in range(128):
        rot[m + 32 if m % 64 < 32 else m - 32, m] = -1.0 if m % 64 < 32 else 1.0
    inv = (f(1.0) / (f(10000.0) ** (np.arange(0, 64, 2, dtype=f) / f(64.0)))).astype(f)
    ang = (np.arange(256, dtype=f)[None, :] * inv[np.arange(128) % 32][:, None]).astype(f)
    a = np.concatenate([ident, rot, np.cos(ang), np.sin(ang)], 1).astype(f)
    mask = np.zeros((2, 512), f)
    mask[0, 0:64], mask[1, 64:128] = 1.0, 1.0
    mask[0, 128 + 64:256] = -1e30
    mask[0, 256:256 + 64], mask[0, 256 + 192:512] = -1e30, -1e30
    mask[1, 256:256 + 128] = -1e30
    return a, mask


def kernel(**inputs):
    import numpy as _np
    import concourse.bacc as _bacc
    from concourse import mybir as _mybir
    from concourse.bass_utils import run_bass_kernel_spmd as _run

    nc = _bacc.Bacc("TRN2", target_bir_lowering=False, num_devices=1)
    consts, mask = _constants()
    arrays, args = {}, []
    for name, a in [(n, inputs[n]) for n in _INS] + [("consts", consts), ("mask", mask)]:
        a = _np.ascontiguousarray(a)
        arrays[f"in_{name}_dram"] = a
        args.append(nc.dram_tensor(f"in_{name}_dram", a.shape, _mybir.dt.from_np(a.dtype), kind="ExternalInput").ap())
    shape = (1, 256, 2048)
    args.append(nc.dram_tensor("out_0_dram", shape, _mybir.dt.float32, kind="ExternalOutput").ap())
    trunk(nc, *args)
    r = _run(nc, [arrays], core_ids=[0])
    return r.results[0]["out_0_dram"]
```
